# Optimizing a Trainium2 kernel written in Bass

```python
import jax, jax.numpy as jnp
from jax import lax
import numpy as np

D_MODEL = 1024
BATCH = 1
SEQ = 256
DEPTH = 1

POOL_WINDOWS = (2, 4, 8, 16)
POOL_GROUPS = 4
POOL_GROUP_DIM = 128
POOL_WIDTH = POOL_GROUPS * POOL_GROUP_DIM
SB_HEADS = 8
SB_HEAD_DIM = 64
SB_WIDTH = SB_HEADS * SB_HEAD_DIM
Q_BLOCK = 128
IN_COLS = POOL_WIDTH + 3 * SB_WIDTH + 2 * D_MODEL
N_EXPERTS = 32
TOP_K = 4
D_EXPERT = D_MODEL
SWIGLU_LIMIT = 7.0
SWIGLU_ALPHA = 1.702
EXPERT_BLOCK = 256
EPS = 1e-6

kernel_name = "hybrid_pool_stickbreaking_moe_block"

def rmsnorm(x, g):
    xf = x.astype(jnp.float32)
    y = xf * lax.rsqrt(jnp.mean(xf * xf, axis=-1, keepdims=True) + EPS)
    return (y * g.astype(jnp.float32)).astype(x.dtype)

def pool_mixer(u, w_pool_grp, pool_scale):
    B, S, _ = u.shape
    uf = u.astype(jnp.float32)
    cs0 = jnp.concatenate([jnp.zeros((B, 1, POOL_WIDTH), jnp.float32), jnp.cumsum(uf, axis=1)], axis=1)
    t = jnp.arange(S)
    pooled = []
    for g, w in enumerate(POOL_WINDOWS):
        c = cs0[..., g * POOL_GROUP_DIM:(g + 1) * POOL_GROUP_DIM]
        upper = c[:, 1:]
        lower = jnp.pad(c, ((0, 0), (w - 1, 0), (0, 0)))[:, :S]
        count = jnp.minimum(t + 1, w).astype(jnp.float32)[None, :, None]
        pooled.append((upper - lower) / count)
    d = (jnp.concatenate(pooled, axis=-1) - uf).reshape(B, S, POOL_GROUPS, POOL_GROUP_DIM)
    mixed = jnp.einsum('bsgc,gcd->bsgd', d, w_pool_grp.astype(jnp.float32)).reshape(B, S, POOL_WIDTH)
    return (mixed * pool_scale.astype(jnp.float32)).astype(u.dtype)

def stick_breaking_attention(q, k, v):
    B, H, S, Dh = q.shape
    n_qb = S // Q_BLOCK
    scale = Dh ** -0.5
    kf = k.astype(jnp.float32)
    vf = v.astype(jnp.float32)
    key_pos = jnp.arange(S)

    def block(i):
        start = i * Q_BLOCK
        qb = lax.dynamic_slice_in_dim(q, start, Q_BLOCK, axis=2).astype(jnp.float32)
        z = jnp.einsum('bhqd,bhkd->bhqk', qb, kf) * scale
        q_pos = start + jnp.arange(Q_BLOCK)
        mask = key_pos[None, :] < q_pos[:, None]
        log_beta = jax.nn.log_sigmoid(z)
        log_1mb = jnp.where(mask, log_beta - z, 0.0)
        rem = lax.cumsum(log_1mb, axis=3, reverse=True) - log_1mb
        a = jnp.where(mask, jnp.exp(log_beta + rem), 0.0)
        return jnp.einsum('bhqk,bhkd->bhqd', a, vf)

    out = lax.map(block, jnp.arange(n_qb))
    out = out.transpose(1, 0, 3, 2, 4).reshape(B, S, H * Dh)
    return out.astype(v.dtype)

def moe_ffn(h, w_router, b_router, w_gate_up, b_gate_up, w_down, b_down):
    B, S, D = h.shape
    N = B * S
    hf = h.reshape(N, D)
    logits = hf.astype(jnp.float32) @ w_router.astype(jnp.float32) + b_router.astype(jnp.float32)
    top_val, top_idx = lax.top_k(logits, TOP_K)
    gate = jax.nn.softmax(top_val, axis=-1)

    n_assign = N * TOP_K
    n_blocks = -(-(n_assign + N_EXPERTS * (EXPERT_BLOCK - 1)) // EXPERT_BLOCK)
    n_rows = n_blocks * EXPERT_BLOCK
    flat_e = top_idx.reshape(-1).astype(jnp.int32)
    flat_tok = jnp.repeat(jnp.arange(N, dtype=jnp.int32), TOP_K)
    flat_gate = gate.reshape(-1)
    order = jnp.argsort(flat_e)
    e_sorted = flat_e[order]
    tok_sorted = flat_tok[order]
    gate_sorted = flat_gate[order]
    counts = jnp.bincount(flat_e, length=N_EXPERTS).astype(jnp.int32)
    padded = (counts + EXPERT_BLOCK - 1) // EXPERT_BLOCK * EXPERT_BLOCK
    start_unp = jnp.cumsum(counts) - counts
    padded_end = jnp.cumsum(padded)
    start_pad = padded_end - padded
    dest = start_pad[e_sorted] + (jnp.arange(n_assign, dtype=jnp.int32) - start_unp[e_sorted])
    row_tok = jnp.full((n_rows,), N, jnp.int32).at[dest].set(tok_sorted)
    row_gate = jnp.zeros((n_rows,), jnp.float32).at[dest].set(gate_sorted)
    block_start = jnp.arange(n_blocks, dtype=jnp.int32) * EXPERT_BLOCK
    block_expert = jnp.minimum(jnp.searchsorted(padded_end, block_start, side='right'), N_EXPERTS - 1).astype(jnp.int32)
    h_pad = jnp.concatenate([hf, jnp.zeros((1, D), hf.dtype)], axis=0)

    def step(acc, blk):
        tok, g, e = blk
        xb = h_pad[tok]
        gu = xb @ w_gate_up[e] + b_gate_up[e]
        glu = jnp.minimum(gu[:, :D_EXPERT], SWIGLU_LIMIT)
        lin = jnp.clip(gu[:, D_EXPERT:], -SWIGLU_LIMIT, SWIGLU_LIMIT)
        act = glu * jax.nn.sigmoid(SWIGLU_ALPHA * glu) * (lin + 1.0)
        y = act @ w_down[e] + b_down[e]
        return acc.at[tok].add((y * g[:, None].astype(y.dtype)).astype(acc.dtype)), None

    acc0 = jnp.zeros((N + 1, D), h.dtype)
    acc, _ = lax.scan(step, acc0, (row_tok.reshape(n_blocks, EXPERT_BLOCK),
                                   row_gate.reshape(n_blocks, EXPERT_BLOCK), block_expert))
    return acc[:N].reshape(B, S, D)

def setup_inputs(seed: int = 0) -> dict:
    key = jax.random.key(seed)
    ks = jax.random.split(key, 20)
    f32 = jnp.float32
    nrm = lambda k, shape, fan_in: jax.random.normal(k, shape, f32) * (fan_in ** -0.5)
    L = DEPTH
    return {
        "x": jax.random.normal(ks[0], (BATCH, SEQ, D_MODEL), f32),
        "norm1_g": 1.0 + 0.05 * jax.random.normal(ks[1], (L, D_MODEL), f32),
        "w_in": nrm(ks[2], (L, D_MODEL, IN_COLS), D_MODEL),
        "q_norm_g": 1.0 + 0.05 * jax.random.normal(ks[3], (L, SB_HEAD_DIM), f32),
        "k_norm_g": 1.0 + 0.05 * jax.random.normal(ks[4], (L, SB_HEAD_DIM), f32),
        "w_pool_grp": nrm(ks[5], (L, POOL_GROUPS, POOL_GROUP_DIM, POOL_GROUP_DIM), POOL_GROUP_DIM),
        "pool_scale": 1.0 + 0.1 * jax.random.normal(ks[6], (L, POOL_WIDTH), f32),
        "w_pool_up": nrm(ks[7], (L, POOL_WIDTH, D_MODEL), POOL_WIDTH),
        "w_attn_up": nrm(ks[8], (L, SB_WIDTH, D_MODEL), SB_WIDTH),
        "w_out": nrm(ks[9], (L, D_MODEL, D_MODEL), D_MODEL),
        "norm2_g": 1.0 + 0.05 * jax.random.normal(ks[10], (L, D_MODEL), f32),
        "w_router": nrm(ks[11], (L, D_MODEL, N_EXPERTS), D_MODEL),
        "b_router": 0.01 * jax.random.normal(ks[12], (L, N_EXPERTS), f32),
        "w_gate_up": nrm(ks[13], (L, N_EXPERTS, D_MODEL, 2 * D_EXPERT), D_MODEL),
        "b_gate_up": 0.01 * jax.random.normal(ks[14], (L, N_EXPERTS, 2 * D_EXPERT), f32),
        "w_down": nrm(ks[15], (L, N_EXPERTS, D_EXPERT, D_MODEL), D_EXPERT),
        "b_down": 0.01 * jax.random.normal(ks[16], (L, N_EXPERTS, D_MODEL), f32),
    }

def reference(x, norm1_g, w_in, q_norm_g, k_norm_g, w_pool_grp, pool_scale, w_pool_up,
              w_attn_up, w_out, norm2_g, w_router, b_router, w_gate_up, b_gate_up,
              w_down, b_down):
    B, S, D = x.shape
    for layer in range(DEPTH):
        h = rmsnorm(x, norm1_g[layer])
        proj = h @ w_in[layer]
        u, q, k, v, g_pool, g_attn = jnp.split(
            proj, [POOL_WIDTH, POOL_WIDTH + SB_WIDTH, POOL_WIDTH + 2 * SB_WIDTH,
                   POOL_WIDTH + 3 * SB_WIDTH, POOL_WIDTH + 3 * SB_WIDTH + D_MODEL], axis=-1)
        q = rmsnorm(q.reshape(B, S, SB_HEADS, SB_HEAD_DIM), q_norm_g[layer]).transpose(0, 2, 1, 3)
        k = rmsnorm(k.reshape(B, S, SB_HEADS, SB_HEAD_DIM), k_norm_g[layer]).transpose(0, 2, 1, 3)
        v = v.reshape(B, S, SB_HEADS, SB_HEAD_DIM).transpose(0, 2, 1, 3)
        pool_out = pool_mixer(u, w_pool_grp[layer], pool_scale[layer]) @ w_pool_up[layer]
        attn_out = stick_breaking_attention(q, k, v) @ w_attn_up[layer]
        merged = jax.nn.sigmoid(g_pool) * pool_out + jax.nn.sigmoid(g_attn) * attn_out
        x = x + merged @ w_out[layer]
        h2 = rmsnorm(x, norm2_g[layer])
        x = x + moe_ffn(h2, w_router[layer], b_router[layer], w_gate_up[layer],
                        b_gate_up[layer], w_down[layer], b_down[layer])
    return x


_drawn_inputs = setup_inputs


def setup_inputs(seed=0):
    import zlib

    import numpy as np

    out = dict(_drawn_inputs(seed))
    spreads = {}
    factors = {'b_router': 3.474, 'b_gate_up': 8.0, 'b_down': 8.0, 'q_norm_g': 3.04}
    for name, (base, spread) in spreads.items():
        noise = np.random.default_rng([zlib.crc32(name.encode()), seed]).standard_normal(out[name].shape)
        drawn = base * np.exp(spread * noise) if base else spread * noise
        out[name] = __import__('jax').numpy.asarray(drawn.astype(out[name].dtype))
    for name, factor in factors.items():
        out[name] = (out[name] * factor).astype(out[name].dtype)
    return out
```

```python
from contextlib import ExitStack

import concourse.bass as bass
from concourse import mybir

P = 128
ALU = mybir.AluOpType
ACT = mybir.ActivationFunctionType
F32 = mybir.dt.float32
BF16 = mybir.dt.bfloat16
I32 = mybir.dt.int32
U32 = mybir.dt.uint32
AX_X = mybir.AxisListType.X

WINDOWS = (2, 4, 8, 16)
TOP_K = 4
LIMIT = 7.0
ALPHA = 1.702
EPS = 1e-6
FAR = 1000.0
MASKED = -1.0e30


def hybrid_block_kernel(nc, x, norm1_g, w_in, q_norm_g, k_norm_g, w_pool_grp, pool_scale, w_pool_up,
                        w_attn_up, w_out, norm2_g, w_router, b_router, w_gate_up, b_gate_up, w_down,
                        b_down, out):
    D = x.shape[2]
    S = x.shape[1]
    T = S // P
    KD = D // P
    E = w_router.shape[2]
    HD = q_norm_g.shape[1]
    HEADS = w_attn_up.shape[1] // HD
    PAIRS = HEADS // 2
    G = len(WINDOWS)
    BLK = 512
    FH = D // 2
    SLOTS = 64
    MAX_OVER = S * TOP_K // SLOTS
    ITEMS = E + MAX_OVER
    COLS = ITEMS + 2
    NSLOT = 2 * KD
    NDOWN = KD // 2
    PAD = max(WINDOWS)
    assert T == 2 and D == 1024 and HD == 64 and HEADS == 8 and G == 4 and E == 32

    x_t = x[0].rearrange("(t p) d -> p t d", p=P)
    out_t = out[0].rearrange("(t p) d -> t p d", p=P)
    w_in_b = w_in[0].rearrange("(k p) (b n) -> b p k n", p=P, n=BLK)

    with ExitStack() as ctx:
        def sb(name, shape, dt=F32):
            return ctx.enter_context(nc.sbuf_tensor(name, shape, dt))

        def sem(name):
            return ctx.enter_context(nc.semaphore(name))

        gate_ring = sb("gate_ring", [P, NSLOT, 2 * D])
        down_ring = sb("down_ring", [P, NDOWN, 2, D])
        area_x = sb("area_x", [P, 2 * D])
        area_m = sb("area_m", [P, 7340])
        bias_up = sb("bias_up", [3 * E, 2 * D], BF16)
        bias_down = sb("bias_down", [3 * E, D], BF16)
        ident = sb("ident", [P, P])
        iota64 = sb("iota64", [P, SLOTS])
        ones_bf = sb("ones_bf", [P, P], BF16)
        below_bf = sb("below_bf", [P, P], BF16)
        cols = sb("cols", [P, 24])
        router_w = sb("router_w", [P, KD, E])
        router_b = sb("router_b", [E, 1])
        tiny = sb("tiny", [P, 64])
        pos_item = sb("pos_item", [P, T, COLS])
        gate_item = sb("gate_item", [P, T, COLS])
        item_sel = sb("item_sel", [3 * E, COLS], BF16)
        sel_item = sb("sel_item", [3 * E, 2, SLOTS], BF16)
        item_table = sb("item_table", [1, COLS + 2], I32)

        def carve(area, lo, *dims, dt=F32):
            n = 1
            for d in dims:
                n *= d
            words = n if dt in (F32, I32, U32) else n // 2
            v = area[:, lo:lo + words]
            if dt != F32:
                v = v.bitcast(dt)
            if len(dims) == 2:
                v = v.rearrange("p (a b) -> p a b", b=dims[1])
            if len(dims) == 3:
                v = v.rearrange("p (a b c) -> p a b c", b=dims[1], c=dims[2])
            return v

        scratch = down_ring[:].rearrange("p a b c -> p (a b c)")
        x_sb = carve(area_x, 0, T, D)
        hT = carve(scratch, 0, KD, S)
        mergedT = carve(scratch, 2048, KD, S)
        kz = carve(scratch, 4096, HEADS, S)
        xn = carve(scratch, 4096, T, D)
        x1 = carve(scratch, 4096, T, D)
        soft = carve(scratch, 6144, 2, 384)
        spos = carve(scratch, 6912, 2, 384)
        esig = carve(scratch, 7680, 2, S)
        rest = carve(scratch, 2048, T, D)
        stage_up = mergedT.rearrange("p a b -> p (a b)")[0:E, :]
        stage_down = scratch[0:E, 6144:6144 + D]
        UW = PAD + S
        uT = carve(area_m, 0, G, UW)
        sumA = carve(area_m, 1088, G, UW)
        sumB = carve(area_m, 2176, G, UW)
        qn = carve(area_m, 1088, T, BLK)
        kn = carve(area_m, 2176, T, BLK)
        attnT = carve(area_m, 1088, PAIRS, S)
        vn = carve(area_m, 3264, T, BLK)
        qT = carve(area_m, 4288, PAIRS, S)
        poolT = carve(area_m, 5312, G, S)
        grp_w = carve(area_m, 6336, G, P)
        from_key = carve(area_m, 6848, P)
        minus = carve(area_m, 6976, P)
        ident_bf = carve(area_m, 7104, P, dt=BF16)
        mask_bf = carve(area_m, 7168, P, dt=BF16)
        inv_count = carve(area_m, 7232, G, PAD)
        attn_prob = carve(area_m, 0, 2, 384)
        mid_part = carve(area_m, 0, 2 * D, dt=BF16)[0:E]
        rows = carve(area_m, 4288, P)
        squares = carve(scratch, 6144, 2, BLK)
        parts = carve(area_m, 0, T, 3 * D, dt=BF16)
        hT_items = carve(area_m, 3072, KD, P)
        y_pair = carve(area_m, 4096, D)
        place_T = carve(area_m, 5120, T, P)
        place_bf = carve(area_m, 5376, T, P, dt=BF16)
        place_g = carve(area_m, 5504, T, P)
        r_lg = carve(area_m, 5760, T, E)
        r_top = carve(area_m, 5824, T, 8)
        r_idx = carve(area_m, 5840, T, 8, dt=U32)
        r_idf = carve(area_m, 5856, T, 8)
        r_p = carve(area_m, 5872, T, 8)
        r_s = carve(area_m, 5888, 8)
        r_eq = carve(area_m, 5896, T * TOP_K, E)
        r_eqp = carve(area_m, 6152, T * TOP_K, E)
        r_sel = carve(area_m, 6408, T, E, dt=BF16)
        r_pos = carve(area_m, 6440, T, E)
        r_iota = carve(area_m, 6504, E)
        o_T = carve(area_m, 6536, 2 * T, P)[0:E]
        o_cnt = carve(area_m, 7048, MAX_OVER)[0:E]
        o_cbf = carve(area_m, 7064, MAX_OVER, dt=BF16)[0:E]
        o_a = carve(area_m, 7072, MAX_OVER)[0:E]
        o_b = carve(area_m, 7088, MAX_OVER)[0:E]
        o_sel = carve(area_m, 7104, 2, MAX_OVER)[0:E]
        o_blk = carve(area_m, 7136, MAX_OVER)[0:E]
        o_j = carve(area_m, 7152, MAX_OVER)[0:E]
        o_e = carve(area_m, 7168, 1)[0:E]
        o_neg = carve(area_m, 7172, P)[0:E]
        o_row = carve(area_m, 7300, 2 * MAX_OVER + 2)[0:1]
        lgT = carve(area_m, 3072, S)[0:E]
        glu = carve(area_x, 0, FH)
        lin = carve(area_x, 512, FH)
        sig = carve(area_x, 1024, FH)
        actT = carve(area_x, 1536, FH // P, P)

        bank = [ctx.enter_context(nc.psum_tensor(f"bank{i}", [P, 512], F32)) for i in range(8)]
        acc, (glu_b, lin_b, y_b, t_b) = bank[0:4], bank[4:8]

        s_x, s_small, s_rw = sem("x_loaded"), sem("small_loaded"), sem("gains_loaded")
        s_bias = sem("biases_loaded")
        names = ["u", "q", "k", "v", "pool_up", "gp0", "gp1", "attn_up", "ga0", "ga1", "out"]
        s_load = {n: sem(f"{n}_loaded") for n in names}
        s_const = sem("constants_done")
        s_pool = sem("pool_order")
        s_dve, s_dve2 = sem("dve_order"), sem("dve_loop_order")
        s_act = sem("act_order")
        s_sumsq, s_mean, s_rstd = sem("sumsq_done"), sem("mean_done"), sem("rstd_done")
        s_xn, s_xT, s_hT = sem("xn_ready"), sem("x_transposed"), sem("hT_ready")
        s_rows, s_cols = sem("rows_transposed"), sem("cols_ready")
        s_proj, s_uT = sem("projected"), sem("u_evacuated")
        s_qkn, s_vn, s_tr, s_qk = sem("qk_normed"), sem("v_ready"), sem("qk_transposed"), sem("qk_ready")
        s_kz0 = sem("kz_zeroed")
        s_dT, s_mix, s_poolT = sem("pool_diff_ready"), sem("pool_mixed"), sem("poolT_ready")
        s_z, s_ln, s_sp = sem("scores_done"), sem("ln_done"), sem("softplus_done")
        s_acc, s_prob, s_o, s_oT = sem("logprob_done"), sem("prob_done"), sem("attn_done"), sem("attnT_ready")
        s_gt, s_esig, s_mrg = sem("gate_tile_done"), sem("gate_exp_done"), sem("merged_ready")
        s_wo, s_x1, s_hn = sem("out_proj_done"), sem("x1_ready"), sem("hn_ready")
        s_hnT, s_hT2 = sem("hn_transposed"), sem("router_in_ready")
        s_lgT, s_lgTs, s_lg = sem("logitsT_done"), sem("logitsT_ready"), sem("logits_done")
        s_soft, s_softe = sem("softmax_in"), sem("softmax_exp")
        s_sel, s_cnt = sem("selection_ready"), sem("ranks_done")
        s_p1, s_rest, s_parts = sem("part_cast"), sem("rest_ready"), sem("parts_ready")
        s_tab, s_tabv = sem("table_matmuls"), sem("table_steps")
        s_bready = sem("biases_split")
        s_table = sem("table_ready")
        s_sela, s_selb = sem("selector_a_ready"), sem("selector_b_ready")
        s_gl = [sem(f"gate_loaded{i}") for i in range(NSLOT)]
        s_dl = [sem(f"down_loaded{i}") for i in range(NDOWN)]
        s_gu, s_du = sem("gate_slots_used"), sem("down_slots_used")
        s_sr, s_glu, s_sig = sem("swiglu_read"), sem("glu_ready"), sem("sigmoid_ready")
        s_actr, s_aps, s_actT = sem("act_ready"), sem("act_transposed"), sem("actT_ready")
        s_y, s_comb = sem("y_ready"), sem("combined")
        s_onehot = sem("one_hot_ready")
        s_place, s_ptp, s_pt = sem("places_ready"), sem("places_transposed"), sem("placeT_ready")
        s_gps, s_gev = sem("gathered"), sem("gather_ready")
        s_final, s_outv, s_outa, s_store = sem("sum_done"), sem("out_by_dve"), sem("out_by_act"), sem("out_stored")

        block = ctx.enter_context(nc.Block())

        def ring_view(slot, n, *dims):
            v = gate_ring[:, slot:slot + n, :].rearrange("p a b -> p (a b)")
            return v.rearrange("p (k n) -> p k n", n=dims[1])

        blk = {"u": 0, "q": 2, "k": 4, "v": 6, "gp0": 10, "gp1": 12, "ga0": 0, "ga1": 2}
        blk = {n: ring_view(s, 2, KD, BLK) for n, s in blk.items()}
        pool_up = ring_view(8, 2, G, D)
        attn_up = ring_view(14, 2, PAIRS, D)
        w_out_sb = ring_view(4, 4, KD, D)
        col_of = {"u": 0, "q": 1, "k": 2, "v": 3, "gp0": 4, "gp1": 5, "ga0": 6, "ga1": 7}
        ROW_G1, ROW_G2, ROW_PS, ROW_Q, ROW_K = 0, KD, 2 * KD, 2 * KD + G, 2 * KD + G + 1
        NROWS = ROW_K + 1

        def head_bank(h):
            return 2 * (h // 2 % 3) + h % 2

        FIRST = (KD, 0)

        @block.sync
        def _(sp):
            sp.dma_start(x_sb, x_t).then_inc(s_x, 16)

            def load_block(n):
                sp.dma_start(blk[n], w_in_b[col_of[n]]).then_inc(s_load[n], 16)

            for n in ("u", "q", "k", "v"):
                load_block(n)
            sp.dma_start(pool_up, w_pool_up[0].rearrange("(k p) n -> p k n", p=P)).then_inc(s_load["pool_up"], 16)
            for n in ("gp0", "gp1"):
                load_block(n)
            sp.dma_start(attn_up, w_attn_up[0].rearrange("(k p) n -> p k n", p=P)).then_inc(s_load["attn_up"], 16)
            sp.wait_ge(s_proj, 1)
            load_block("ga0")
            sp.wait_ge(s_proj, 3)
            load_block("ga1")
            sp.wait_ge(s_proj, 7)
            sp.dma_start(w_out_sb, w_out[0].rearrange("(k p) n -> p k n", p=P)).then_inc(s_load["out"], 16)

            def load_gate(e, half, c):
                sp.dma_start(gate_ring[:, FIRST[half] + c, :], w_gate_up[0, e, c * P:(c + 1) * P, :]) \
                  .then_inc(s_gl[FIRST[half] + c], 16)

            def load_gate_at(e, half, c):
                sp.dma_start(gate_ring[:, FIRST[half] + c, :],
                             w_gate_up[0, bass.ds(e, 1), c * P:(c + 1) * P, :].rearrange("a p n -> (a p) n")) \
                  .then_inc(s_gl[FIRST[half] + c], 16)

            def down_src(e, c):
                return w_down[0, bass.ds(e, 1), 2 * c * P:2 * (c + 1) * P, :] \
                    .rearrange("a (k p) n -> p (a k) n", p=P)

            for c in range(KD):
                if c == 0:
                    sp.wait_ge(s_gt, KD)
                if c == 6:
                    sp.wait_ge(s_gt, 2 * KD)
                load_gate(0, 0, c)
            for c in range(4):
                load_gate(1, 1, c)
            sp.wait_ge(s_wo, 1)
            for c in range(4, KD):
                load_gate(1, 1, c)
            sp.wait_ge(s_lgT, 1)
            sp.wait_ge(s_parts, T)
            for c in range(NDOWN):
                sp.dma_start(down_ring[:, c], w_down[0, 0, 2 * c * P:2 * (c + 1) * P, :]
                             .rearrange("(k p) n -> p k n", p=P)).then_inc(s_dl[c], 16)
            for c in range(NDOWN):
                sp.wait_ge(s_du, c + 1)
                sp.dma_start(down_ring[:, c], w_down[0, 1, 2 * c * P:2 * (c + 1) * P, :]
                             .rearrange("(k p) n -> p k n", p=P)).then_inc(s_dl[c], 16)
            sp.wait_ge(s_table, 1)
            pairs = sp.value_load(item_table[0:1, COLS:COLS + 1], min_val=E // 2, max_val=ITEMS // 2)
            with sp.Fori(1, pairs) as i:
                for half in range(2):
                    e = sp.value_load(item_table[0:1, bass.ds(2 * i + half, 1)], min_val=0, max_val=E - 1)
                    for c in range(KD):
                        sp.wait_ge(s_gu, (i - 1) * (2 * KD) + (half * KD + c + 1))
                        load_gate_at(e, half, c)
                    for c in range(NDOWN):
                        sp.wait_ge(s_du, i * (2 * NDOWN) + ((half - 1) * NDOWN + c + 1))
                        sp.dma_start(down_ring[:, c], down_src(e, c)).then_inc(s_dl[c], 16)
            for t in range(T):
                for n in range(2):
                    sp.wait_ge((s_outv, s_outa)[n], t + 1)
                    sp.dma_start(out_t[t, :, n * FH:(n + 1) * FH], gate_ring[:, 2 * t + n, 0:FH]) \
                      .then_inc(s_store, 16)
            sp.wait_ge(s_store, 16 * 2 * T)

        @block.gpsimd
        def _(pool):
            order = [0]

            def link(ins):
                order[0] += 1
                ins.then_inc(s_pool, 1)
                pool.wait_ge(s_pool, order[0])

            consts = [0]

            def const(ins):
                consts[0] += 1
                ins.then_inc(s_const, 1)
                pool.wait_ge(s_const, consts[0])

            def select(view, compare, fill, mult=1, step=-1, base=0, n=P):
                return nc.gpsimd.affine_select(out=view, in_=view, compare_op=compare, fill=fill, base=base,
                                               pattern=[[step, n]], channel_multiplier=mult)

            def power(dst, src, n):
                return nc.gpsimd.tensor_tensor(dst, src, tiny[:, 62:63].to_broadcast([P, n]), ALU.pow)

            link(nc.gpsimd.memset(ident[:], 0.0))
            const(select(ident[:], ALU.not_equal, 1.0))
            link(nc.gpsimd.memset(tiny[:, 62:63], -0.5))
            pool.wait_ge(s_mean, 1)
            power(tiny[:, 4:6], tiny[:, 2:4], T).then_inc(s_rstd, 1)
            pool.wait_ge(s_rstd, 1)
            link(nc.gpsimd.memset(mask_bf, 0.0))
            const(select(mask_bf, ALU.is_gt, MASKED, mult=-1, step=1))
            link(nc.gpsimd.memset(ident_bf, 0.0))
            const(select(ident_bf, ALU.not_equal, 1.0))
            link(nc.gpsimd.memset(from_key, -1.0))
            const(select(from_key, ALU.is_ge, 0.0))
            const(nc.gpsimd.memset(minus, -1.0))
            const(nc.gpsimd.memset(ones_bf[:], 1.0))
            link(nc.gpsimd.memset(below_bf[:], 1.0))
            const(select(below_bf[:], ALU.is_gt, 0.0, mult=-1, step=1))
            const(nc.gpsimd.iota(iota64[:], pattern=[[1, SLOTS]], base=0, channel_multiplier=0,
                                 allow_small_or_imprecise_dtypes=True))
            link(nc.gpsimd.memset(item_sel[:], 0.0))
            for part in range(3):
                v = item_sel[part * E:(part + 1) * E, 0:E]
                const(select(v, ALU.not_equal, 1.0, n=E))
            const(nc.gpsimd.iota(item_table[:], pattern=[[1, COLS + 2]], base=0, channel_multiplier=0))
            pool.wait_ge(s_xT, 1)
            nc.gpsimd.memset(kz, 0.0).then_inc(s_kz0, 1)
            pool.wait_ge(s_kz0, 1)
            for n in range(2):
                pool.wait_ge(s_mean, 2 + n)
                power(tiny[:, 16 + 16 * n:32 + 16 * n], tiny[:, 16 + 16 * n:32 + 16 * n], 2 * HEADS) \
                    .then_inc(s_rstd, 1)
                pool.wait_ge(s_rstd, 2 + n)
            pool.wait_ge(s_mean, 4)
            power(tiny[:, 4:6], tiny[:, 2:4], T).then_inc(s_rstd, 1)
            pool.wait_ge(s_rstd, 4)
            pool.wait_ge(s_mix, 1)
            for t in range(T):
                pool.wait_ge(s_p1, t + 1)
                nc.gpsimd.tensor_tensor(rest[:, t], x1[:, t], parts[:, t, 0:D], ALU.subtract) \
                    .then_inc(s_rest, 1)
                pool.wait_ge(s_rest, t + 1)
            for t in range(T):
                pool.wait_ge(s_p1, T + t + 1)
                nc.gpsimd.tensor_tensor(parts[:, t, 2 * D:3 * D], rest[:, t], parts[:, t, D:2 * D], ALU.subtract) \
                    .then_inc(s_parts, 1)
                pool.wait_ge(s_parts, t + 1)
            const(nc.gpsimd.iota(r_iota, pattern=[[1, E]], base=0, channel_multiplier=0,
                                 allow_small_or_imprecise_dtypes=True))
            const(nc.gpsimd.iota(o_j, pattern=[[1, MAX_OVER]], base=0, channel_multiplier=0,
                                 allow_small_or_imprecise_dtypes=True))
            const(nc.gpsimd.iota(o_e, pattern=[[0, 1]], base=0, channel_multiplier=1,
                                 allow_small_or_imprecise_dtypes=True))
            const(nc.gpsimd.memset(o_neg, -1.0))
            const(nc.gpsimd.memset(place_T, 0.0))
            nc.gpsimd.memset(y_pair, 0.0).then_inc(s_y, 1)

        N_CONST = 17

        @block.scalar
        def _(act):
            row_src = [(ROW_G1, norm1_g[0].rearrange("(k p) -> k p", p=P)),
                       (ROW_G2, norm2_g[0].rearrange("(k p) -> k p", p=P)),
                       (ROW_PS, pool_scale[0].rearrange("(k p) -> k p", p=P))]
            for r, src in row_src:
                act.dma_start(rows[r:r + src.shape[0], :], src).then_inc(s_rw, 16)
            for r, src in ((ROW_Q, q_norm_g), (ROW_K, k_norm_g)):
                for half in range(2):
                    act.dma_start(rows[r:r + 1, half * HD:(half + 1) * HD], src).then_inc(s_rw, 16)
            act.dma_start(stage_up, b_gate_up[0]).then_inc(s_bias, 16)
            act.dma_start(stage_down, b_down[0]).then_inc(s_bias, 16)
            act.dma_start(grp_w, w_pool_grp[0].rearrange("g c d -> c g d")).then_inc(s_small, 16)
            act.dma_start(router_w[:], w_router[0].rearrange("(k p) e -> p k e", p=P)).then_inc(s_small, 16)
            act.dma_start(router_b[:], b_router[0].rearrange("(e a) -> e a", a=1)).then_inc(s_small, 16)

            act.wait_ge(s_x, 16)
            for t in range(T):
                last = nc.scalar.activation(hT.rearrange("p a b -> p (a b)")[:, t * D:(t + 1) * D], x_sb[:, t],
                                            ACT.Square, accum_out=tiny[:, t:t + 1])
            last.then_inc(s_sumsq, 1)
            act.wait_ge(s_bready, 1)
            act.wait_ge(s_cols, 1)
            for n in range(2):
                for t in range(T):
                    act.wait_ge(s_proj, 2 + 2 * n + t)
                    if n:
                        act.wait_ge(s_mean, 2)
                    nc.scalar.activation(squares[:, t], bank[(6, 0)[n] + t][:], ACT.Square).then_inc(s_sumsq, 1)
            for t in range(T):
                act.wait_ge(s_proj, 6 + t)
                nc.scalar.activation(vn[:, t], bank[2 + t][:], ACT.Copy).then_inc(s_vn, 1)

            for t in range(2 * KD):
                if 0 <= t - 1 < PAIRS:
                    for h in (2 * (t - 1), 2 * (t - 1) + 1):
                        act.wait_ge(s_acc, h + 1)
                        if h >= 2:
                            act.wait_ge(s_o, h - 1)
                        nc.scalar.activation(attn_prob[:, h % 2], bank[head_bank(h)][:, 0:384], ACT.Exp) \
                            .then_inc(s_prob, 1)
                if t < PAIRS:
                    for h in (2 * t, 2 * t + 1):
                        act.wait_ge(s_z, h + 1)
                        if h >= 2:
                            act.wait_ge(s_sp, h - 1)
                        nc.scalar.activation(soft[:, h % 2], bank[head_bank(h)][:, 0:384], ACT.Abs).then_inc(s_act, 1)
                        act.wait_ge(s_act, 2 * h + 1)
                        nc.scalar.activation(soft[:, h % 2], soft[:, h % 2], ACT.Exp, scale=-1.0).then_inc(s_act, 1)
                        act.wait_ge(s_act, 2 * h + 2)
                        nc.scalar.activation(soft[:, h % 2], soft[:, h % 2], ACT.Ln, bias=1.0).then_inc(s_ln, 1)
                if 0 <= t - 2 < PAIRS:
                    for h in (2 * (t - 2), 2 * (t - 2) + 1):
                        act.wait_ge(s_o, h + 1)
                        half = h % 2
                        nc.scalar.activation(attnT[half * HD:(half + 1) * HD, h // 2, :],
                                             bank[head_bank(h)][half * HD:(half + 1) * HD, 0:S], ACT.Copy) \
                            .then_inc(s_oT, 1)
                act.wait_ge(s_gt, t + 1)
                if t >= 2:
                    act.wait_ge(s_mrg, t - 1)
                nc.scalar.activation(esig[:, t % 2], bank[6 + t % 2][:, 0:S], ACT.Exp, scale=-1.0) \
                    .then_inc(s_esig, 1)

            for t in range(T):
                act.wait_ge(s_x1, t + 1)
                nc.scalar.activation(rest[:, t], x1[:, t], ACT.Square, accum_out=tiny[:, t:t + 1]) \
                    .then_inc(s_sumsq, 1)
            for t in range(T):
                act.wait_ge(s_hn, t + 1)
                nc.scalar.activation(parts[:, t, 0:D], x1[:, t], ACT.Copy).then_inc(s_p1, 1)
            for t in range(T):
                act.wait_ge(s_rest, t + 1)
                nc.scalar.activation(parts[:, t, D:2 * D], rest[:, t], ACT.Copy).then_inc(s_p1, 1)
            act.wait_ge(s_soft, 1)
            nc.scalar.activation(r_p, r_p, ACT.Exp).then_inc(s_softe, 1)

            act.wait_ge(s_table, 1)
            pairs = act.value_load(item_table[0:1, COLS:COLS + 1], min_val=E // 2, max_val=ITEMS // 2)
            with act.Fori(0, pairs) as i:
                for half in range(2):
                    act.wait_ge(s_glu, 2 * i + (half + 1))
                    nc.scalar.activation(sig, glu, ACT.Sigmoid, scale=ALPHA).then_inc(s_sig, 1)
                    if half == 0:
                        act.wait_ge(s_ptp, i + 1)
                        act.wait_ge(s_comb, i + 1)
                        nc.scalar.activation(place_T.rearrange("p a b -> p (a b)"), y_b[:, 0:T * P], ACT.Copy) \
                            .then_inc(s_pt, 1)
                    act.wait_ge(s_du, (2 * i + (half + 1)) * NDOWN)
                    for c in range(2):
                        last = nc.scalar.activation(y_pair[half * SLOTS:(half + 1) * SLOTS, c * FH:(c + 1) * FH],
                                                    y_b[c * SLOTS:(c + 1) * SLOTS, :], ACT.Copy)
                    last.then_inc(s_y, 1)
            for t in range(T):
                act.wait_ge(s_final, 2 * t + 2)
                nc.scalar.activation(gate_ring[:, 2 * t + 1, 0:FH], acc[2 * t + 1][:], ACT.Copy).then_inc(s_outa, 1)

        @block.vector
        def _(dve):
            order = [0]

            def link(ins):
                order[0] += 1
                ins.then_inc(s_dve, 1)
                dve.wait_ge(s_dve, order[0])

            def tt(o, a, b, op):
                return nc.vector.tensor_tensor(o, a, b, op)

            def mean(n, view, width):
                nc.vector.tensor_scalar(view[0], view[1], 1.0 / width, EPS, ALU.mult, ALU.add).then_inc(s_mean, 1)

            for v in (uT, sumA, sumB):
                nc.vector.memset(v[:, :, 0:PAD], 0.0)
            for g, w in enumerate(WINDOWS):
                for t in range(PAD):
                    if t < w:
                        nc.vector.memset(inv_count[:, g, t:t + 1], 1.0 / (t + 1))
                if w < PAD:
                    nc.vector.memset(inv_count[:, g, w:PAD], 1.0 / w)
            link(nc.vector.memset(tiny[:, 63:64], 0.0))
            dve.wait_ge(s_sumsq, 1)
            mean(0, (tiny[:, 2:4], tiny[:, 0:2]), D)
            dve.wait_ge(s_rstd, 1)
            for t in range(T):
                nc.vector.tensor_scalar(xn[:, t], x_sb[:, t], tiny[:, 4 + t:5 + t], None, ALU.mult) \
                    .then_inc(s_xn, 1)
            dve.wait_ge(s_rows, 1)
            nc.vector.tensor_copy(cols[:, 0:NROWS], bank[4][:, 0:NROWS]).then_inc(s_cols, 1)
            dve.wait_ge(s_cols, 1)
            dve.wait_ge(s_xT, 1)
            for b in range(4):
                tt(hT[:, 2 * b:2 * b + 2, :], bank[b][:].rearrange("p (a n) -> p a n", n=S),
                   cols[:, ROW_G1 + 2 * b:ROW_G1 + 2 * b + 2].unsqueeze(2).to_broadcast([P, 2, S]), ALU.mult) \
                    .then_inc(s_hT, 1)
            dve.wait_ge(s_bias, 32)
            for stage, dst in ((stage_up, bias_up), (stage_down, bias_down)):
                mid = mid_part[:, 0:stage.shape[1]]
                link(nc.vector.tensor_copy(dst[0:E, :], stage))
                link(tt(stage, stage, dst[0:E, :], ALU.subtract))
                link(nc.vector.tensor_copy(mid, stage))
                link(nc.vector.tensor_copy(dst[E:2 * E, :], mid))
                link(tt(stage, stage, mid, ALU.subtract))
                link(nc.vector.tensor_copy(dst[2 * E:3 * E, :], stage))
            nc.vector.memset(tiny[:, 63:64], 0.0).then_inc(s_bready, 1)

            for b in range(2):
                dve.wait_ge(s_proj, 1)
                link(nc.vector.tensor_copy(uT[:, 2 * b:2 * b + 2, PAD:],
                                           bank[4 + b][:].rearrange("p (a n) -> p a n", n=S)))
            src = uT
            for level in range(G):
                dst = (sumA, sumB)[level % 2]
                step = 1 << level
                link(tt(dst[:, level:, PAD:], src[:, level:, PAD:], src[:, level:, PAD - step:UW - step], ALU.add))
                src = dst
            for g, w in enumerate(WINDOWS):
                s = (sumA, sumB)[g % 2][:, g]
                link(tt(s[:, 0:PAD], s[:, PAD:2 * PAD], inv_count[:, g, :], ALU.mult))
                nc.vector.scalar_tensor_tensor(out=uT[:, g, 2 * PAD:], in0=s[:, 2 * PAD:], scalar=1.0 / w,
                                               in1=uT[:, g, 2 * PAD:], op0=ALU.mult, op1=ALU.subtract)
                link(tt(uT[:, g, PAD:2 * PAD], s[:, 0:PAD], uT[:, g, PAD:2 * PAD], ALU.subtract))
            nc.vector.memset(tiny[:, 63:64], 0.0).then_inc(s_dT, 1)

            for n, dst in enumerate((qn, kn)):
                v = tiny[:, 16 + 16 * n:32 + 16 * n]
                for t in range(T):
                    dve.wait_ge(s_sumsq, 2 + 2 * n + t)
                    link(nc.vector.tensor_reduce(v[:, t * HEADS:(t + 1) * HEADS],
                                                 squares[:, t].rearrange("p (h d) -> p h d", d=HD), AX_X, ALU.add))
                mean(1 + n, (v, v), HD)
                dve.wait_ge(s_rstd, 2 + n)
                for t in range(T):
                    tt(dst[:, t].rearrange("p (h d) -> p h d", d=HD),
                       bank[(6, 0)[n] + t][:].rearrange("p (h d) -> p h d", d=HD),
                       v[:, t * HEADS:(t + 1) * HEADS].unsqueeze(2).to_broadcast([P, HEADS, HD]), ALU.mult) \
                        .then_inc(s_qkn, 1)
            for b in range(2):
                dve.wait_ge(s_mix, 1)
                tt(poolT[:, 2 * b:2 * b + 2, :], bank[4 + b][:].rearrange("p (a n) -> p a n", n=S),
                   cols[:, ROW_PS + 2 * b:ROW_PS + 2 * b + 2].unsqueeze(2).to_broadcast([P, 2, S]), ALU.mult) \
                    .then_inc(s_poolT, 1)
            for b in range(2):
                dve.wait_ge(s_tr, 1)
                nc.vector.tensor_scalar(qT[:, 2 * b:2 * b + 2, :], bank[6 + b][:].rearrange("p (a n) -> p a n", n=S),
                                        cols[:, ROW_Q:ROW_Q + 1], float(HD) ** -0.5, ALU.mult, ALU.mult) \
                    .then_inc(s_qk, 1)
            dve.wait_ge(s_tr, 2)
            dve.wait_ge(s_kz0, 1)
            kz_v = kz.rearrange("p (a h) n -> p a h n", h=2)
            for b in range(2):
                for half in range(2):
                    r = slice(half * HD, (half + 1) * HD)
                    nc.vector.tensor_scalar(kz_v[r, 2 * b:2 * b + 2, half, :],
                                            bank[b][r, :].rearrange("p (a n) -> p a n", n=S),
                                            cols[r, ROW_K:ROW_K + 1], None, ALU.mult).then_inc(s_qk, 1)

            for t in range(2 * KD):
                if t < PAIRS:
                    for h in (2 * t, 2 * t + 1):
                        dve.wait_ge(s_ln, h + 1)
                        if h >= 2:
                            dve.wait_ge(s_acc, h - 1)
                        nc.vector.scalar_tensor_tensor(out=spos[:, h % 2], in0=bank[head_bank(h)][:, 0:384],
                                                       scalar=0.0, in1=soft[:, h % 2], op0=ALU.max,
                                                       op1=ALU.add).then_inc(s_sp, 1)
                dve.wait_ge(s_esig, t + 1)
                e = esig[:, t % 2]
                link(nc.vector.tensor_scalar(e, e, 1.0, None, ALU.add))
                link(nc.vector.reciprocal(e, e))
                if t < KD:
                    tt(mergedT[:, t], bank[6 + t % 2][:, S:2 * S], e, ALU.mult).then_inc(s_mrg, 1)
                else:
                    link(tt(e, bank[6 + t % 2][:, S:2 * S], e, ALU.mult))
                    tt(mergedT[:, t - KD], mergedT[:, t - KD], e, ALU.add).then_inc(s_mrg, 1)

            dve.wait_ge(s_wo, 1)
            for t in range(T):
                for n in range(2):
                    last = tt(x1[:, t, n * FH:(n + 1) * FH], acc[2 * t + n][:], x_sb[:, t, n * FH:(n + 1) * FH],
                              ALU.add)
                last.then_inc(s_x1, 1)
            dve.wait_ge(s_sumsq, 7)
            mean(3, (tiny[:, 2:4], tiny[:, 0:2]), D)
            dve.wait_ge(s_rstd, 4)
            for t in range(T):
                nc.vector.tensor_scalar(x1[:, t], x1[:, t], tiny[:, 4 + t:5 + t], None, ALU.mult).then_inc(s_hn, 1)
            dve.wait_ge(s_hnT, 1)
            for b in range(4):
                tt(hT[:, 2 * b:2 * b + 2, :], bank[4 + b][:].rearrange("p (a n) -> p a n", n=S),
                   cols[:, ROW_G2 + 2 * b:ROW_G2 + 2 * b + 2].unsqueeze(2).to_broadcast([P, 2, S]), ALU.mult) \
                    .then_inc(s_hT2, 1)
            dve.wait_ge(s_lgT, 1)
            nc.vector.tensor_scalar(lgT, bank[4][0:E, 0:S], router_b[:, 0:1], None, ALU.add).then_inc(s_lgTs, 1)
            dve.wait_ge(s_lg, 1)
            link(nc.vector.tensor_copy(r_lg, bank[5][:, 0:T * E].rearrange("p (t e) -> p t e", e=E)))
            for t in range(T):
                link(nc.vector.max(r_top[:, t], r_lg[:, t]))
            for t in range(T):
                last = nc.vector.max_index(r_idx[:, t], r_top[:, t], r_lg[:, t])
            link(last)
            tt(r_p, r_top, r_top[:, :, 0:1].to_broadcast([P, T, 8]), ALU.subtract).then_inc(s_soft, 1)
            link(nc.vector.tensor_copy(r_idf, r_idx))
            dve.wait_ge(s_const, N_CONST)
            eq4 = r_eq.rearrange("p (t r) e -> p t r e", r=TOP_K)
            eqp4 = r_eqp.rearrange("p (t r) e -> p t r e", r=TOP_K)
            for t in range(T):
                last = tt(eq4[:, t], r_iota.unsqueeze(1).to_broadcast([P, TOP_K, E]),
                          r_idf[:, t, 0:TOP_K].unsqueeze(2).to_broadcast([P, TOP_K, E]), ALU.is_equal)
            link(last)
            with nc.allow_low_precision(reason="sums of four zeros and ones, at most one of them a one"):
                nc.vector.tensor_reduce(r_sel, eq4.rearrange("p t r e -> p t e r"), AX_X, ALU.add).then_inc(s_sel, 1)
            dve.wait_ge(s_softe, 1)
            link(nc.vector.tensor_reduce(r_s[:, 0:T], r_p[:, :, 0:TOP_K], AX_X, ALU.add))
            link(nc.vector.reciprocal(r_s[:, 0:T], r_s[:, 0:T]))
            link(tt(r_p, r_p, r_s[:, 0:T].unsqueeze(2).to_broadcast([P, T, 8]), ALU.mult))
            for t in range(T):
                last = tt(eqp4[:, t], eq4[:, t], r_p[:, t, 0:TOP_K].unsqueeze(2).to_broadcast([P, TOP_K, E]), ALU.mult)
            link(last)
            link(nc.vector.tensor_reduce(gate_item[:, :, 0:E], eqp4.rearrange("p t r e -> p t e r"), AX_X, ALU.add))
            dve.wait_ge(s_cnt, 1)
            link(nc.vector.scalar_tensor_tensor(out=r_pos, in0=bank[6][:, 0:T * E].rearrange("p (t e) -> p t e", e=E),
                                                scalar=FAR, in1=r_sel, op0=ALU.add, op1=ALU.mult))
            nc.vector.memset(pos_item[:, :, ITEMS:], -FAR)
            nc.vector.memset(gate_item[:, :, ITEMS:], 0.0)
            link(nc.vector.tensor_scalar(pos_item[:, :, 0:E], r_pos, FAR, None, ALU.subtract))

            def places(at):
                iota4 = iota64[:].unsqueeze(1).to_broadcast([P, 2, SLOTS])
                for t in range(T):
                    tt(place_bf[:, t].rearrange("p (j s) -> p j s", s=SLOTS), iota4,
                       pos_item[:, t, at].unsqueeze(2).to_broadcast([P, 2, SLOTS]), ALU.is_equal) \
                        .then_inc(s_onehot, 1)
                return at

            def gated(at):
                for t in range(T):
                    last = tt(place_g[:, t].rearrange("p (j s) -> p j s", s=SLOTS),
                              place_bf[:, t].rearrange("p (j s) -> p j s", s=SLOTS),
                              gate_item[:, t, at].unsqueeze(2).to_broadcast([P, 2, SLOTS]), ALU.mult)
                last.then_inc(s_place, 1)

            def selector(half, col, signal):
                nc.vector.tensor_copy(sel_item[:, half, :], item_sel[:, col].to_broadcast([3 * E, SLOTS])) \
                    .then_inc(signal, 1)

            def evacuate_gather(r):
                src = (t_b, y_b)[r][:].rearrange("p (a n) -> p a n", n=P)
                g = cols[:, ROW_G2 + 4 * r:ROW_G2 + 4 * r + 4].unsqueeze(2).to_broadcast([P, 4, P])
                tt(hT_items[:, 4 * r:4 * r + 4, :], src, g, ALU.mult).then_inc(s_gev, 1)

            places(slice(0, 2))
            dve.wait_ge(s_onehot, T)
            gated(slice(0, 2))
            selector(0, slice(0, 1), s_sela)
            for r in range(2):
                dve.wait_ge(s_gps, r + 1)
                evacuate_gather(r)

            dve.wait_ge(s_tab, 1)
            nc.vector.tensor_copy(o_T, glu_b[0:E, :].rearrange("p (a n) -> p a n", n=P))
            cnt = lin_b[0:E, 0:MAX_OVER]
            link(nc.vector.tensor_scalar(o_cnt, cnt, float(SLOTS), None, ALU.is_gt))
            for m in (2, 3):
                link(nc.vector.scalar_tensor_tensor(out=o_cnt, in0=cnt, scalar=float(m * SLOTS), in1=o_cnt,
                                                    op0=ALU.is_gt, op1=ALU.add))
            nc.vector.tensor_copy(o_cbf, o_cnt).then_inc(s_tabv, 1)
            dve.wait_ge(s_tab, 2)
            link(tt(o_a, o_j, lin_b[0:E, 64:64 + MAX_OVER], ALU.subtract))
            link(tt(o_b, o_a, o_cnt, ALU.is_lt))
            link(nc.vector.scalar_tensor_tensor(out=o_sel[:, 0], in0=o_a, scalar=0.0, in1=o_b, op0=ALU.is_ge,
                                                op1=ALU.mult))
            link(nc.vector.scalar_tensor_tensor(out=o_blk, in0=o_a, scalar=1.0, in1=o_sel[:, 0], op0=ALU.add,
                                                op1=ALU.mult))
            link(nc.vector.tensor_scalar(o_blk, o_blk, float(SLOTS), None, ALU.mult))
            link(nc.vector.tensor_scalar(o_sel[:, 1], o_sel[:, 0], o_e[:, 0:1], None, ALU.mult))
            for part in range(3):
                nc.vector.tensor_copy(item_sel[part * E:(part + 1) * E, E:ITEMS], o_sel[:, 0])
            nc.vector.memset(tiny[:, 63:64], 0.0).then_inc(s_tabv, 1)
            dve.wait_ge(s_tab, 3)
            nc.vector.tensor_scalar(pos_item[:, :, E:ITEMS], glu_b[:, 0:T * MAX_OVER]
                                    .rearrange("p (t j) -> p t j", t=T), FAR, None, ALU.subtract)
            nc.vector.tensor_copy(gate_item[:, :, E:ITEMS], glu_b[:, T * MAX_OVER:2 * T * MAX_OVER]
                                  .rearrange("p (t j) -> p t j", t=T))
            row = lin_b[0:1, 128:128 + 2 * MAX_OVER]
            nc.vector.tensor_scalar(item_table[0:1, E:ITEMS], row[:, MAX_OVER:2 * MAX_OVER], -1.0, None, ALU.mult)
            link(nc.vector.tensor_reduce(o_row[:, 0:1], row[:, 0:MAX_OVER].rearrange("p (a b) -> p b a", b=2)[:, 0, :],
                                         AX_X, ALU.add))
            nc.vector.tensor_scalar(item_table[0:1, COLS:COLS + 1], o_row[:, 0:1], -1.0, float(E // 2),
                                    ALU.mult, ALU.add).then_inc(s_table, 1)
            nc.vector.memset(tiny[:, 63:64], 0.0).then_inc(s_sr, 1)

            dve.wait_ge(s_table, 1)
            pairs = dve.value_load(item_table[0:1, COLS:COLS + 1], min_val=E // 2, max_val=ITEMS // 2)
            with dve.Fori(0, pairs) as i:
                for half in range(2):
                    n1 = 2 * i + (half + 1)
                    dve.wait_ge(s_gu, n1 * KD)
                    nc.vector.tensor_scalar(glu, glu_b[:], LIMIT, None, ALU.min).then_inc(s_glu, 1)
                    nc.vector.tensor_scalar(lin, lin_b[:], LIMIT, -LIMIT, ALU.min, ALU.max).then_inc(s_sr, 1)
                    dve.wait_ge(s_glu, n1)
                    dve.wait_ge(s_sr, n1 + 1)
                    nc.vector.scalar_tensor_tensor(out=lin, in0=lin, scalar=1.0, in1=glu, op0=ALU.add,
                                                   op1=ALU.mult).then_inc(s_dve2, 1)
                    if half == 1:
                        dve.wait_ge(s_gps, 2 * i + 3)
                        evacuate_gather(0)
                    dve.wait_ge(s_dve2, n1)
                    dve.wait_ge(s_sig, n1)
                    tt(lin, lin, sig, ALU.mult).then_inc(s_actr, 1)
                    if half == 1:
                        dve.wait_ge(s_gps, 2 * i + 4)
                        evacuate_gather(1)
                    dve.wait_ge(s_aps, n1)
                    nc.vector.tensor_copy(actT, t_b[:].rearrange("p (a n) -> p a n", n=P)).then_inc(s_actT, 1)
                    if half == 0:
                        selector(1, bass.ds(2 * i + 1, 1), s_selb)
                        dve.wait_ge(s_ptp, i + 1)
                        ahead = bass.ds(2 * i + 2, 2)
                        places(ahead)
                        dve.wait_ge(s_onehot, T * i + 2 * T)
                        gated(ahead)
                    else:
                        selector(0, bass.ds(2 * i + 2, 1), s_sela)
            for t in range(T):
                dve.wait_ge(s_final, 2 * t + 1)
                nc.vector.tensor_copy(gate_ring[:, 2 * t, 0:FH], acc[2 * t][:]).then_inc(s_outv, 1)

        @block.tensor
        def _(pe):
            def mm(o, lhsT, rhs, start):
                return nc.tensor.matmul(o, lhsT, rhs, start=start, stop=True, skip_group_check=True)

            pe.wait_ge(s_const, 1)
            pe.wait_ge(s_rw, 16 * 7)
            nc.tensor.transpose(bank[4][:, 0:NROWS], rows[0:NROWS], ident[0:NROWS, 0:NROWS]).then_inc(s_rows, 1)
            pe.wait_ge(s_xn, T)
            for k in range(KD):
                for t in range(T):
                    last = nc.tensor.transpose(bank[k // 2][:, (k % 2) * S + t * P:(k % 2) * S + (t + 1) * P],
                                               xn[:, t, k * P:(k + 1) * P], ident[:])
            last.then_inc(s_xT, 1)
            pe.wait_ge(s_load["u"], 16)
            pe.wait_ge(s_cols, 1)
            for g in range(G):
                for k in range(KD):
                    pe.wait_ge(s_hT, k // 2 + 1) if g == 0 and k % 2 == 0 else None
                    last = mm(bank[4 + g // 2][:, (g % 2) * S:(g % 2 + 1) * S], blk["u"][:, k, g * P:(g + 1) * P],
                              hT[:, k, :], k == 0)
            last.then_inc(s_proj, 1)
            for n, b in (("q", 6), ("k", 0), ("v", 2)):
                pe.wait_ge(s_load[n], 16)
                for t in range(T):
                    for k in range(KD):
                        last = mm(bank[b + t][:], hT[:, k, t * P:(t + 1) * P], blk[n][:, k, :], k == 0)
                    last.then_inc(s_proj, 1)
            pe.wait_ge(s_dT, 1)
            pe.wait_ge(s_small, 16 * 3)
            for g in range(G):
                last = mm(bank[4 + g // 2][:, (g % 2) * S:(g % 2 + 1) * S], grp_w[:, g, :], uT[:, g, PAD:], True)
            last.then_inc(s_mix, 1)
            for n, (src, b) in enumerate(((qn, 6), (kn, 0))):
                pe.wait_ge(s_qkn, T * (n + 1))
                for a in range(PAIRS):
                    for t in range(T):
                        last = nc.tensor.transpose(
                            bank[b + a // 2][:, (a % 2) * S + t * P:(a % 2) * S + (t + 1) * P],
                            src[:, t, a * P:(a + 1) * P], ident[:])
                last.then_inc(s_tr, 1)

            pe.wait_ge(s_const, 7)
            pe.wait_ge(s_poolT, 2)
            pe.wait_ge(s_qk, 6)
            pe.wait_ge(s_vn, T)
            for t in range(2 * KD):
                if 0 <= t - 2 < PAIRS:
                    for h in (2 * (t - 2), 2 * (t - 2) + 1):
                        pe.wait_ge(s_prob, h + 1)
                        half = h % 2
                        o = bank[head_bank(h)][half * HD:(half + 1) * HD, :]
                        mm(o[:, 0:S], vn[:, 0, h * HD:(h + 1) * HD], attn_prob[:, half, 0:S], True)
                        mm(o[:, P:S], vn[:, 1, h * HD:(h + 1) * HD], attn_prob[:, half, S:S + P], False) \
                            .then_inc(s_o, 1)
                if 0 <= t - 1 < PAIRS:
                    for h in (2 * (t - 1), 2 * (t - 1) + 1):
                        pe.wait_ge(s_sp, h + 1)
                        o, s = bank[head_bank(h)], spos[:, h % 2]
                        mm(o[:, 0:S], from_key, s[:, 0:S], False)
                        mm(o[:, P:S], minus, s[:, S:S + P], False)
                        mm(o[:, S:S + P], from_key, s[:, S:S + P], False).then_inc(s_acc, 1)
                if t < PAIRS:
                    if t >= 3:
                        pe.wait_ge(s_oT, 2 * (t - 3) + 2)
                    for h in (2 * t, 2 * t + 1):
                        o = bank[head_bank(h)]
                        mm(o[:, 0:S], kz[:, h, 0:P], qT[:, h // 2, :], True)
                        mm(o[:, S:S + P], kz[:, h, P:S], qT[:, h // 2, P:S], False)
                        mm(o[:, 0:P], ident_bf, mask_bf, False)
                        mm(o[:, S:S + P], ident_bf, mask_bf, False).then_inc(s_z, 1)
                which, d = ("gp", "ga")[t // KD], t % KD
                w = f"{which}{d // 4}"
                up, src = ((pool_up, poolT), (attn_up, attnT))[t // KD]
                if d % 4 == 0:
                    pe.wait_ge(s_load[w], 16)
                if d == 0:
                    pe.wait_ge(s_load[("pool_up", "attn_up")[t // KD]], 16)
                if t == KD:
                    pe.wait_ge(s_oT, HEADS)
                if t >= 2:
                    pe.wait_ge(s_mrg, t - 1)
                o = bank[6 + t % 2]
                for k in range(KD):
                    mm(o[:, 0:S], blk[w][:, k, (d % 4) * P:(d % 4 + 1) * P], hT[:, k, :], k == 0)
                for k in range(G):
                    last = mm(o[:, S:2 * S], up[:, k, d * P:(d + 1) * P], src[:, k, :], False)
                last.then_inc(s_gt, 1)
            pe.wait_ge(s_load["out"], 16)
            for k in range(KD):
                pe.wait_ge(s_mrg, KD + k + 1)
                for t in range(T):
                    for n in range(2):
                        last = mm(acc[2 * t + n][:], mergedT[:, k, t * P:(t + 1) * P],
                                  w_out_sb[:, k, n * FH:(n + 1) * FH], k == 0)
            last.then_inc(s_wo, 1)
            for t in range(T):
                pe.wait_ge(s_hn, t + 1)
                for k in range(KD):
                    last = nc.tensor.transpose(bank[4 + k // 2][:, (k % 2) * S + t * P:(k % 2) * S + (t + 1) * P],
                                               x1[:, t, k * P:(k + 1) * P], ident[:])
            last.then_inc(s_hnT, 1)
            for k in range(KD):
                if k % 2 == 0:
                    pe.wait_ge(s_hT2, 4 if k == 0 else k // 2 + 1)
                last = mm(bank[4][0:E, 0:S], router_w[:, k, :], hT[:, k, :], k == 0)
            last.then_inc(s_lgT, 1)
            pe.wait_ge(s_lgTs, 1)
            for t in range(T):
                last = nc.tensor.transpose(bank[5][:, t * E:(t + 1) * E], lgT[:, t * P:(t + 1) * P], ident[0:E, 0:E])
            last.then_inc(s_lg, 1)
            pe.wait_ge(s_x1, T)
            for t in range(T):
                for n in range(2):
                    mm(acc[2 * t + n][:], ident[:], x_sb[:, t, n * FH:(n + 1) * FH], False)
            pe.wait_ge(s_sel, 1)
            mm(bank[6][:, 0:E], below_bf[:], r_sel[:, 0], True)
            mm(bank[6][:, E:2 * E], ones_bf[:], r_sel[:, 0], False)
            mm(bank[6][:, E:2 * E], below_bf[:], r_sel[:, 1], False).then_inc(s_cnt, 1)

            def gather(r):
                o = (t_b, y_b)[r]
                for k in range(4 * r, 4 * r + 4):
                    for t in range(T):
                        for part in range(3):
                            last = mm(o[:, (k % 4) * P:(k % 4 + 1) * P],
                                      parts[:, t, part * D + k * P:part * D + (k + 1) * P], place_bf[:, t, :],
                                      k == 4 * r and t == 0 and part == 0)
                last.then_inc(s_gps, 1)

            pe.wait_ge(s_parts, T)
            pe.wait_ge(s_place, 1)
            for r in range(2):
                gather(r)

            for t in range(T):
                nc.tensor.transpose(glu_b[0:E, t * P:(t + 1) * P], r_pos[:, t], ident[:])
                nc.tensor.transpose(glu_b[0:E, (T + t) * P:(T + t + 1) * P], gate_item[:, t, 0:E], ident[:])
            for t in range(T):
                last = mm(lin_b[0:E, 0:MAX_OVER], r_sel[:, t], ones_bf[:, 0:MAX_OVER], t == 0)
            last.then_inc(s_tab, 1)
            pe.wait_ge(s_tabv, 1)
            mm(lin_b[0:E, 64:64 + MAX_OVER], below_bf[0:E, 0:E], o_cbf, True).then_inc(s_tab, 1)
            pe.wait_ge(s_tabv, 2)
            for t in range(T):
                v = glu_b[:, t * MAX_OVER:(t + 1) * MAX_OVER]
                mm(v, o_T[:, t, :], o_sel[:, 0], t == 0)
                mm(v, o_neg, o_blk, False)
                mm(glu_b[:, (T + t) * MAX_OVER:(T + t + 1) * MAX_OVER], o_T[:, T + t, :], o_sel[:, 0], False)
            mm(lin_b[0:1, 128:128 + 2 * MAX_OVER], o_neg[:, 0:1], o_sel.rearrange("p a b -> p (a b)"), True) \
                .then_inc(s_tab, 1)

            def combine():
                for t in range(T):
                    for n in range(2):
                        yield mm(acc[2 * t + n][:], place_T[:, t, :], y_pair[:, n * FH:(n + 1) * FH], False)

            pe.wait_ge(s_table, 1)
            pe.wait_ge(s_const, N_CONST)
            pairs = pe.value_load(item_table[0:1, COLS:COLS + 1], min_val=E // 2, max_val=ITEMS // 2)
            with pe.Fori(0, pairs) as i:
                for half in range(2):
                    n0 = 2 * i + half
                    slots = slice(half * SLOTS, (half + 1) * SLOTS)
                    if half == 0:
                        pe.wait_ge(s_gev, 2 * i + 2)
                        pe.wait_ge(s_sela, i + 1)
                    else:
                        pe.wait_ge(s_selb, i + 1)
                    pe.wait_ge(s_sr, n0 + 1)
                    for c in range(2):
                        for b, m in ((glu_b, 0), (lin_b, 1)):
                            lo = m * D + c * FH
                            mm(b[c * SLOTS:(c + 1) * SLOTS, :], sel_item[:, half, :], bias_up[:, lo:lo + FH], True)
                    for k in range(KD):
                        s = FIRST[half] + k
                        pe.wait_ge(s_gl[s], 16 * i + 16)
                        for b, m in ((glu_b, 0), (lin_b, 1)):
                            for c in range(2):
                                lo = m * D + c * FH
                                last = mm(b[c * SLOTS:(c + 1) * SLOTS, :], hT_items[:, k, slots],
                                          gate_ring[:, s, lo:lo + FH], False)
                        last.then_inc(s_gu, 1)
                    if half == 0:
                        pe.wait_ge(s_y, 2 * i + 1)
                        for last in combine():
                            pass
                        last.then_inc(s_comb, 1)
                        pe.wait_ge(s_place, i + 1)
                        for t in range(T):
                            last = nc.tensor.transpose(y_b[:, t * P:(t + 1) * P], place_g[:, t], ident[:])
                        last.then_inc(s_ptp, 1)
                    else:
                        pe.wait_ge(s_place, i + 2)
                        gather(0)
                        pe.wait_ge(s_y, 2 * i + 2)
                        gather(1)
                        pe.wait_ge(s_gev, 2 * i + 3)
                    pe.wait_ge(s_actr, n0 + 1)
                    for c in range(FH // P):
                        last = nc.tensor.transpose(t_b[:, c * P:(c + 1) * P], lin[:, c * P:(c + 1) * P], ident[:])
                    last.then_inc(s_aps, 1)
                    if half == 0:
                        pe.wait_ge(s_pt, i + 1)
                    else:
                        pe.wait_ge(s_gev, 2 * i + 4)
                    for c in range(2):
                        mm(y_b[c * SLOTS:(c + 1) * SLOTS, :], sel_item[:, half, :], bias_down[:, c * FH:(c + 1) * FH],
                           True)
                    pe.wait_ge(s_actT, n0 + 1)
                    for k in range(KD):
                        if k % 2 == 0:
                            pe.wait_ge(s_dl[k // 2], 32 * i + 16 * (half + 1))
                        f0 = (k // 4) * SLOTS
                        for c in range(2):
                            last = mm(y_b[c * SLOTS:(c + 1) * SLOTS, :], actT[:, k % 4, f0:f0 + SLOTS],
                                      down_ring[:, k // 2, k % 2, c * FH:(c + 1) * FH], False)
                        if k % 2:
                            last.then_inc(s_du, 1)
            pe.wait_ge(s_y, 2 * pairs + 1)
            for last in combine():
                last.then_inc(s_final, 1)


_INS = ["x", "norm1_g", "w_in", "q_norm_g", "k_norm_g", "w_pool_grp", "pool_scale", "w_pool_up", "w_attn_up",
        "w_out", "norm2_g", "w_router", "b_router", "w_gate_up", "b_gate_up", "w_down", "b_down"]


def kernel(**inputs):
    import numpy as _np
    import concourse.bacc as _bacc
    from concourse import mybir as _mybir
    from concourse.bass_utils import run_bass_kernel_spmd as _run

    nc = _bacc.Bacc("TRN2", target_bir_lowering=False, num_devices=1)
    arrays, args = {}, []
    for name in _INS:
        a = _np.ascontiguousarray(inputs[name])
        arrays[f"in_{name}_dram"] = a
        args.append(nc.dram_tensor(f"in_{name}_dram", a.shape, _mybir.dt.from_np(a.dtype),
                                   kind="ExternalInput").ap())
    out = nc.dram_tensor("out_0_dram", inputs["x"].shape, _mybir.dt.float32, kind="ExternalOutput").ap()
    hybrid_block_kernel(nc, *args, out)
    r = _run(nc, [arrays], core_ids=[0])
    return r.results[0]["out_0_dram"]
```

```python
from contextlib import ExitStack

import concourse.bass as bass
from concourse import mybir

P = 128
ALU = mybir.AluOpType
ACT = mybir.ActivationFunctionType
F32 = mybir.dt.float32
F32R = mybir.dt.float32r
BF16 = mybir.dt.bfloat16
I32 = mybir.dt.int32
U32 = mybir.dt.uint32
AX_X = mybir.AxisListType.X

WINDOWS = (2, 4, 8, 16)
TOP_K = 4
LIMIT = 7.0
ALPHA = 1.702
EPS = 1e-6
FAR = 1000.0
MASKED = -1.0e30


def hybrid_block_kernel(nc, x, norm1_g, w_in, q_norm_g, k_norm_g, w_pool_grp, pool_scale, w_pool_up,
                        w_attn_up, w_out, norm2_g, w_router, b_router, w_gate_up, b_gate_up, w_down,
                        b_down, out):
    D = x.shape[2]
    S = x.shape[1]
    T = S // P
    KD = D // P
    E = w_router.shape[2]
    HD = q_norm_g.shape[1]
    HEADS = w_attn_up.shape[1] // HD
    PAIRS = HEADS // 2
    G = len(WINDOWS)
    BLK = 512
    FH = D // 2
    SLOTS = 64
    MAX_OVER = S * TOP_K // SLOTS
    ITEMS = E + MAX_OVER
    COLS = ITEMS + 2
    NSLOT = 2 * KD
    NDOWN = KD // 2
    PAD = max(WINDOWS)
    EARLY = 5
    assert T == 2 and D == 1024 and HD == 64 and HEADS == 8 and G == 4 and E == 32

    x_t = x[0].rearrange("(t p) d -> p t d", p=P)
    out_t = out[0].rearrange("(t p) d -> t p d", p=P)
    w_in_b = w_in[0].rearrange("(k p) (b n) -> b p k n", p=P, n=BLK)

    with ExitStack() as ctx:
        def sb(name, shape, dt=F32):
            return ctx.enter_context(nc.sbuf_tensor(name, shape, dt))

        def sem(name):
            return ctx.enter_context(nc.semaphore(name))

        ring_at = (nc.sbuf_base + 31) // 32 * 32
        gate_ring = sb("gate_ring", [P, NSLOT, 2 * D])
        scratch_at = (nc.sbuf_base + 31) // 32 * 32
        down_ring = sb("down_ring", [P, NDOWN, 2, D])
        area_x = sb("area_x", [P, 2 * D])
        area_m = sb("area_m", [P, 7360])
        bias_up = sb("bias_up", [3 * E, 2 * D], BF16)
        bias_down = sb("bias_down", [3 * E, D], BF16)
        ident = sb("ident", [P, P])
        iota64 = sb("iota64", [P, SLOTS])
        ones_bf = sb("ones_bf", [P, P], BF16)
        below_bf = sb("below_bf", [P, P], BF16)
        cols = sb("cols", [P, 24])
        router_w = sb("router_w", [P, KD, E])
        router_b = sb("router_b", [P, E])
        tiny = sb("tiny", [P, 64])
        pos_item = sb("pos_item", [P, T, COLS])
        gate_item = sb("gate_item", [P, T, COLS])
        item_sel = sb("item_sel", [3 * E, COLS], BF16)
        sel_item = sb("sel_item", [3 * E, 2, SLOTS], BF16)
        item_table = sb("item_table", [1, COLS + 2], I32)

        def carve(area, lo, *dims, dt=F32):
            n = 1
            for d in dims:
                n *= d
            words = n if dt in (F32, I32, U32) else n // 2
            v = area[:, lo:lo + words]
            if dt != F32:
                v = v.bitcast(dt)
            if len(dims) == 2:
                v = v.rearrange("p (a b) -> p a b", b=dims[1])
            if len(dims) == 3:
                v = v.rearrange("p (a b c) -> p a b c", b=dims[1], c=dims[2])
            return v

        NRAW, NHI, BW = 5, 2, KD * BLK
        HI_AT, PR_AT = 6, 5

        def buffer(name, at, dt):
            return nc.alloc_sbuf_tensor_at(name, [P, BW], dt, offset=ring_at + at * BW * 4)

        raw = [buffer(f"raw{j}", j, F32) for j in range(NRAW)]
        w_lo = [buffer(f"w_lo{j}", j, F32R) for j in range(NRAW)]
        w_hi = [buffer(f"w_hi{j}", HI_AT + j, F32R) for j in range(NHI)]
        mix_in = nc.alloc_sbuf_tensor_at("mix_in", [P, 2, 2, PAIRS, S], F32R, offset=ring_at + PR_AT * BW * 4)
        act_in = nc.alloc_sbuf_tensor_at("act_in", [P, 2, KD, S], F32R, offset=scratch_at)
        w_hi_f = [w[:].bitcast(F32) for w in w_hi]
        mix_f = mix_in[:].rearrange("p a b c n -> p (a b) (c n)").bitcast(F32)

        scratch = down_ring[:].rearrange("p a b c -> p (a b c)")
        x_sb = carve(area_x, 0, T, D)
        act_f = act_in[:].rearrange("p a k n -> p a (k n)").bitcast(F32)
        hT = carve(scratch, 0, KD, S)
        kz = carve(scratch, 4096, HEADS, S)
        xn = carve(scratch, 4096, T, D)
        x1 = carve(scratch, 4096, T, D)
        squares = carve(scratch, 6144, 2, BLK)
        soft = carve(scratch, 6144, 2, 384)
        spos = carve(scratch, 6912, 2, 384)
        rest = carve(scratch, 2048, T, D)
        UW = PAD + S
        uT = carve(area_m, 0, G, UW)
        rows = carve(area_m, 0, P)
        mid_part = carve(area_m, 0, 2 * D, dt=BF16)[0:E]
        qn = carve(area_m, 1088, T, BLK)
        kn = carve(area_m, 2176, T, BLK)
        sumA = carve(area_m, 1088, G, UW)
        sumB = carve(area_m, 2176, G, UW)
        gate_p = carve(area_m, 1088, KD, S)
        stage_up = carve(area_m, 3264, 2 * D)[0:E]
        vn = carve(area_m, 3264, T, BLK)
        qT = carve(area_m, 4288, PAIRS, S)
        stage_down = carve(area_m, 5312, D)[0:E]
        attn_prob = carve(area_m, 5312, 2, 384)
        gate_a = carve(area_m, 5312, KD, S)
        grp_w = carve(area_m, 6336, G, P)
        from_key = carve(area_m, 6848, P)
        minus = carve(area_m, 6976, P)
        ident_bf = carve(area_m, 7104, P, dt=BF16)
        mask_bf = carve(area_m, 7168, P, dt=BF16)
        inv_count = carve(area_m, 7232, G, PAD)
        parts = carve(area_m, 0, T, 3 * D, dt=BF16)
        hT_items = carve(area_m, 3072, KD, P)
        y_pair = carve(area_m, 4096, D)
        place_T = carve(area_m, 5120, T, P)
        place_bf = carve(area_m, 5376, T, P, dt=BF16)
        place_g = carve(area_m, 5504, T, P)
        r_lg = carve(area_m, 5760, T, E)
        r_top = carve(area_m, 5824, T, 8)
        r_idx = carve(area_m, 5840, T, 8, dt=U32)
        r_idf = carve(area_m, 5856, T, 8)
        r_p = carve(area_m, 5872, T, 8)
        r_s = carve(area_m, 5888, 8)
        r_eq = carve(area_m, 5896, T * TOP_K, E)
        r_eqp = carve(area_m, 6152, T * TOP_K, E)
        r_sel = carve(area_m, 6408, T, E, dt=BF16)
        r_pos = carve(area_m, 6440, T, E)
        r_iota = carve(area_m, 6504, E)
        o_T = carve(area_m, 6536, 2 * T, P)[0:E]
        o_cnt = carve(area_m, 7048, MAX_OVER)[0:E]
        o_cbf = carve(area_m, 7064, MAX_OVER, dt=BF16)[0:E]
        o_a = carve(area_m, 7072, MAX_OVER)[0:E]
        o_b = carve(area_m, 7088, MAX_OVER)[0:E]
        o_sel = carve(area_m, 7104, 2, MAX_OVER)[0:E]
        o_blk = carve(area_m, 7136, MAX_OVER)[0:E]
        o_j = carve(area_m, 7152, MAX_OVER)[0:E]
        o_e = carve(area_m, 7168, 1)[0:E]
        o_neg = carve(area_m, 7172, P)[0:E]
        o_row = carve(area_m, 7300, 2 * MAX_OVER + 2)[0:1]
        lgT = carve(area_m, 3072, S)[0:E]
        glu = carve(area_x, 0, FH)
        lin = carve(area_x, 512, FH)
        sig = carve(area_x, 1024, FH)
        actT = carve(area_x, 1536, FH // P, P)

        bank = [ctx.enter_context(nc.psum_tensor(f"bank{i}", [P, 512], F32)) for i in range(8)]
        acc, (glu_b, lin_b, y_b, t_b) = bank[0:4], bank[4:8]

        s_x, s_small, s_rw = sem("x_loaded"), sem("small_loaded"), sem("gains_loaded")
        s_bias = sem("biases_loaded")
        BLOCKS = ["q", "k", "v", "u", "gp0", "gp1", "pool_up", "ga0", "ga1", "attn_up", "out0", "out1"]
        s_load = {n: sem(f"{n}_loaded") for n in BLOCKS}
        s_hi, s_lo = sem("first_parts_done"), sem("rests_done")
        s_unit, s_ev, s_ga = sem("unit_done"), sem("unit_evacuated"), sem("attn_gate_ready")
        s_sigp, s_half, s_mf, s_mhi = sem("pool_gate_ready"), sem("mix_hi"), sem("merged_sum"), sem("merged_hi")
        s_const = sem("constants_done")
        s_pool = sem("pool_order")
        s_dve, s_dve2 = sem("dve_order"), sem("dve_loop_order")
        s_act = sem("act_order")
        s_sumsq, s_mean, s_rstd = sem("sumsq_done"), sem("mean_done"), sem("rstd_done")
        s_xn, s_xT, s_hTh, s_hT = sem("xn_ready"), sem("x_transposed"), sem("hT_hi"), sem("hT_ready")
        s_rows, s_cols = sem("rows_transposed"), sem("cols_ready")
        s_proj = sem("projected")
        s_qkn, s_vn, s_tr, s_qk = sem("qk_normed"), sem("v_ready"), sem("qk_transposed"), sem("qk_ready")
        s_kz0 = sem("kz_zeroed")
        s_dT = sem("pool_diff_ready")
        s_z, s_ln, s_sp = sem("scores_done"), sem("ln_done"), sem("softplus_done")
        s_acc, s_prob, s_o = sem("logprob_done"), sem("prob_done"), sem("attn_done")
        s_oh, s_oT, s_mrg = sem("attnT_hi"), sem("attnT_ready"), sem("merged_ready")
        s_wo, s_x1, s_hn = sem("out_proj_done"), sem("x1_ready"), sem("hn_ready")
        s_hnT, s_hT2, s_hT3 = sem("x1_transposed"), sem("router_in_by_dve"), sem("router_in_by_act")
        s_lgT, s_lgTs, s_lg = sem("logitsT_done"), sem("logitsT_ready"), sem("logits_done")
        s_soft, s_softe = sem("softmax_in"), sem("softmax_exp")
        s_sel, s_cnt = sem("selection_ready"), sem("ranks_done")
        s_p1, s_rest, s_parts = sem("part_cast"), sem("rest_ready"), sem("parts_ready")
        s_tab, s_tabv = sem("table_matmuls"), sem("table_steps")
        s_bready = sem("biases_split")
        s_table, s_ids = sem("pairs_counted"), sem("experts_listed")
        s_sela, s_selb = sem("selector_a_ready"), sem("selector_b_ready")
        s_gl = [sem(f"gate_loaded{i}") for i in range(NSLOT)]
        s_dl = [sem(f"down_loaded{i}") for i in range(NDOWN)]
        s_gu, s_du = sem("gate_slots_used"), sem("down_slots_used")
        s_sr, s_glu, s_sig = sem("swiglu_read"), sem("glu_ready"), sem("sigmoid_ready")
        s_actr, s_aps, s_actT = sem("act_ready"), sem("act_transposed"), sem("actT_ready")
        s_y, s_comb = sem("y_ready"), sem("combined")
        s_onehot = sem("one_hot_ready")
        s_place, s_ptp, s_pt = sem("places_ready"), sem("places_transposed"), sem("placeT_ready")
        s_gps, s_gev = sem("gathered"), sem("gather_ready")
        s_final, s_outv, s_outa, s_store = sem("sum_done"), sem("out_by_dve"), sem("out_by_act"), sem("out_stored")

        block = ctx.enter_context(nc.Block())

        col_of = {"u": 0, "q": 1, "k": 2, "v": 3, "gp0": 4, "gp1": 5, "ga0": 6, "ga1": 7}
        ROW_G1, ROW_G2, ROW_PS, ROW_Q, ROW_K = 0, KD, 2 * KD, 2 * KD + G, 2 * KD + G + 1
        NROWS = ROW_K + 1

        UNITS = [("u", 0), ("u", 1), ("gp0", 0), ("gp0", 1), ("mix", 0), ("mix", 1), ("gp1", 0), ("gp1", 1)] \
            + [("pool_up", j) for j in range(4)] + [("ga0", 0), ("ga0", 1), ("ga1", 0), ("ga1", 1)] \
            + [("attn_up", j) for j in range(4)]
        STEP = {0: 0, 1: 1, 2: 2, 3: 3, 6: 4, 7: 5}

        def used(b):
            return {0: (s_proj, 2), 1: (s_proj, 4), 2: (s_proj, 6), 3: (s_unit, 2), 4: (s_unit, 4), 5: (s_unit, 8),
                    6: (s_unit, 12), 7: (s_unit, 14), 8: (s_unit, 16), 9: (s_unit, 20), 10: (s_wo, 2),
                    11: (s_wo, 4)}[b]

        SPLIT_AT = {2: 5, 4: 6, 8: 7, 12: 8, 14: 9, 16: 10}

        def pieces(b):
            n = 4 if b == 0 else 2
            before = 0 if b == 0 else 4 + 2 * (b - 1)
            return [(i * BW // n, BW // n, before + i + 1) for i in range(n)]

        def unit_wait(eng, n):
            if UNITS[n][0].startswith("ga"):
                eng.wait_ge(s_ga, n - 11)
            else:
                eng.wait_ge(s_ev, n + 1 if n < 12 else n - 3)

        def head_bank(h):
            return 2 * (h // 2 % 3) + h % 2

        SLOT = ((4, 5, 6, 7, 8, 9, 10, 11), (0, 1, 12, 13, 2, 3, 14, 15))

        @block.sync
        def _(sp):
            sp.dma_start(x_sb, x_t).then_inc(s_x, 16)

            def load_block(b):
                n = BLOCKS[b]
                if b >= NRAW:
                    sp.wait_ge(*used(b - NRAW))
                if n in col_of:
                    src = w_in_b[col_of[n]]
                elif n.startswith("out"):
                    src = w_out[0].rearrange("(k p) (b n) -> b p k n", p=P, n=BLK)[int(n[3])]
                else:
                    src = {"pool_up": w_pool_up, "attn_up": w_attn_up}[n][0].rearrange("(k p) n -> p k n", p=P)
                sp.dma_start(raw[b % NRAW][:].rearrange("p (k n) -> p k n", n=src.shape[2]), src) \
                  .then_inc(s_load[n], 16)

            for r, src in ((ROW_G1, norm1_g), (ROW_G2, norm2_g), (ROW_PS, pool_scale)):
                n = src.shape[1] // P
                sp.dma_start(rows[r:r + n, :], src[0].rearrange("(k p) -> k p", p=P)).then_inc(s_rw, 16)
            load_block(0)
            sp.dma_start(grp_w, w_pool_grp[0].rearrange("g c d -> c g d")).then_inc(s_small, 16)
            sp.dma_start(stage_up, b_gate_up[0]).then_inc(s_bias, 16)
            sp.dma_start(stage_down, b_down[0]).then_inc(s_bias, 16)
            for b in range(1, NRAW):
                load_block(b)
            sp.dma_start(router_w[:], w_router[0].rearrange("(k p) e -> p k e", p=P)).then_inc(s_small, 16)
            sp.dma_start(router_b[:], b_router[0:1, :].to_broadcast([P, E])).then_inc(s_small, 16)
            for b in range(NRAW, len(BLOCKS)):
                load_block(b)

            def load_gate(e, half, c):
                s = SLOT[half][c]
                sp.dma_start(gate_ring[:, s, :], w_gate_up[0, e, c * P:(c + 1) * P, :]).then_inc(s_gl[s], 16)

            def load_gate_at(e, half, c):
                s = SLOT[half][c]
                sp.dma_start(gate_ring[:, s, :],
                             w_gate_up[0, bass.ds(e, 1), c * P:(c + 1) * P, :].rearrange("a p n -> (a p) n")) \
                  .then_inc(s_gl[s], 16)

            def load_down(e, c):
                sp.dma_start(down_ring[:, c], w_down[0, e, 2 * c * P:2 * (c + 1) * P, :]
                             .rearrange("(k p) n -> p k n", p=P)).then_inc(s_dl[c], 16)

            def down_src(e, c):
                return w_down[0, bass.ds(e, 1), 2 * c * P:2 * (c + 1) * P, :] \
                    .rearrange("a (k p) n -> p (a k) n", p=P)

            for c in range(KD):
                if c % 2 == 0:
                    sp.wait_ge(*used((7, 8, 9, 9)[c // 2]))
                load_gate(0, 0, c)
            for c in range(KD):
                if c % 4 == 0:
                    sp.wait_ge(*used((10, 11)[c // 4]))
                load_gate(1, 1, c)
            sp.wait_ge(s_lgT, 1)
            sp.wait_ge(s_parts, T)
            for c in range(NDOWN):
                load_down(0, c)
            with sp.Fori(1, EARLY) as i:
                for half in range(2):
                    for c in range(KD):
                        sp.wait_ge(s_gu, (i - 1) * (2 * KD) + (half * KD + c + 1))
                        load_gate_at(2 * i + half, half, c)
                    for c in range(NDOWN):
                        sp.wait_ge(s_du, (i - 1) * (2 * NDOWN) + (half * NDOWN + c + 1))
                        sp.dma_start(down_ring[:, c], down_src(2 * i + half - 1, c)).then_inc(s_dl[c], 16)
            for c in range(NDOWN):
                sp.wait_ge(s_du, (2 * EARLY - 2) * NDOWN + c + 1)
                load_down(2 * EARLY - 1, c)
            sp.wait_ge(s_ids, 1)
            pairs = sp.value_load(item_table[0:1, COLS:COLS + 1], min_val=E // 2, max_val=ITEMS // 2)
            with sp.Fori(EARLY, pairs) as i:
                for half in range(2):
                    e = sp.value_load(item_table[0:1, bass.ds(2 * i + half, 1)], min_val=0, max_val=E - 1)
                    for c in range(KD):
                        sp.wait_ge(s_gu, (i - 1) * (2 * KD) + (half * KD + c + 1))
                        load_gate_at(e, half, c)
                    for c in range(NDOWN):
                        sp.wait_ge(s_du, i * (2 * NDOWN) + ((half - 1) * NDOWN + c + 1))
                        sp.dma_start(down_ring[:, c], down_src(e, c)).then_inc(s_dl[c], 16)
            for t in range(T):
                for n in range(2):
                    sp.wait_ge((s_outv, s_outa)[n], t + 1)
                    sp.dma_start(out_t[t, :, n * FH:(n + 1) * FH], gate_ring[:, 2 * t + n, 0:FH]) \
                      .then_inc(s_store, 16)
            sp.wait_ge(s_store, 16 * 2 * T)

        @block.gpsimd
        def _(pool):
            order = [0]

            def link(ins):
                order[0] += 1
                ins.then_inc(s_pool, 1)
                pool.wait_ge(s_pool, order[0])

            consts = [0]

            def const(ins):
                consts[0] += 1
                ins.then_inc(s_const, 1)
                pool.wait_ge(s_const, consts[0])

            def select(view, compare, fill, mult=1, step=-1, base=0, n=P):
                return nc.gpsimd.affine_select(out=view, in_=view, compare_op=compare, fill=fill, base=base,
                                               pattern=[[step, n]], channel_multiplier=mult)

            def power(dst, src, n):
                return nc.gpsimd.tensor_tensor(dst, src, tiny[:, 62:63].to_broadcast([P, n]), ALU.pow)

            link(nc.gpsimd.memset(ident[:], 0.0))
            const(select(ident[:], ALU.not_equal, 1.0))
            link(nc.gpsimd.memset(tiny[:, 62:63], -0.5))
            pool.wait_ge(s_mean, 1)
            power(tiny[:, 4:6], tiny[:, 2:4], T).then_inc(s_rstd, 1)
            pool.wait_ge(s_rstd, 1)
            link(nc.gpsimd.memset(mask_bf, 0.0))
            const(select(mask_bf, ALU.is_gt, MASKED, mult=-1, step=1))
            link(nc.gpsimd.memset(ident_bf, 0.0))
            const(select(ident_bf, ALU.not_equal, 1.0))
            link(nc.gpsimd.memset(from_key, -1.0))
            const(select(from_key, ALU.is_ge, 0.0))
            const(nc.gpsimd.memset(minus, -1.0))
            const(nc.gpsimd.memset(ones_bf[:], 1.0))
            link(nc.gpsimd.memset(below_bf[:], 1.0))
            const(select(below_bf[:], ALU.is_gt, 0.0, mult=-1, step=1))
            const(nc.gpsimd.iota(iota64[:], pattern=[[1, SLOTS]], base=0, channel_multiplier=0,
                                 allow_small_or_imprecise_dtypes=True))
            link(nc.gpsimd.memset(item_sel[:], 0.0))
            for part in range(3):
                v = item_sel[part * E:(part + 1) * E, 0:E]
                const(select(v, ALU.not_equal, 1.0, n=E))
            const(nc.gpsimd.iota(item_table[:], pattern=[[1, COLS + 2]], base=0, channel_multiplier=0))
            pool.wait_ge(s_xT, 1)
            nc.gpsimd.memset(kz, 0.0).then_inc(s_kz0, 1)
            pool.wait_ge(s_kz0, 1)
            for n in range(2):
                pool.wait_ge(s_mean, 2 + n)
                power(tiny[:, 16 + 16 * n:32 + 16 * n], tiny[:, 16 + 16 * n:32 + 16 * n], 2 * HEADS) \
                    .then_inc(s_rstd, 1)
                pool.wait_ge(s_rstd, 2 + n)
            pool.wait_ge(s_mean, 4)
            power(tiny[:, 4:6], tiny[:, 2:4], T).then_inc(s_rstd, 1)
            pool.wait_ge(s_rstd, 4)
            pool.wait_ge(s_wo, 2 * T)
            const(nc.gpsimd.iota(r_iota, pattern=[[1, E]], base=0, channel_multiplier=0,
                                 allow_small_or_imprecise_dtypes=True))
            const(nc.gpsimd.iota(o_j, pattern=[[1, MAX_OVER]], base=0, channel_multiplier=0,
                                 allow_small_or_imprecise_dtypes=True))
            const(nc.gpsimd.iota(o_e, pattern=[[0, 1]], base=0, channel_multiplier=1,
                                 allow_small_or_imprecise_dtypes=True))
            const(nc.gpsimd.memset(o_neg, -1.0))
            const(nc.gpsimd.memset(place_T, 0.0))
            nc.gpsimd.memset(y_pair, 0.0).then_inc(s_y, 1)
            pool.wait_ge(s_y, 1)
            for t in range(T):
                pool.wait_ge(s_p1, T + t + 1)
                nc.gpsimd.tensor_tensor(parts[:, t, 2 * D:3 * D], rest[:, t], parts[:, t, D:2 * D], ALU.subtract) \
                    .then_inc(s_parts, 1)
                pool.wait_ge(s_parts, t + 1)

        N_CONST = 17

        @block.scalar
        def _(act):
            for r, src in ((ROW_Q, q_norm_g), (ROW_K, k_norm_g)):
                for half in range(2):
                    act.dma_start(rows[r:r + 1, half * HD:(half + 1) * HD], src).then_inc(s_rw, 16)

            act.wait_ge(s_x, 16)
            for t in range(T):
                last = nc.scalar.activation(hT.rearrange("p a b -> p (a b)")[:, t * D:(t + 1) * D], x_sb[:, t],
                                            ACT.Square, accum_out=tiny[:, t:t + 1])
            last.then_inc(s_sumsq, 1)

            def split(b):
                if b >= NHI:
                    act.wait_ge(*used(b - NHI))
                act.wait_ge(s_load[BLOCKS[b]], 16)
                for lo, n, _ in pieces(b):
                    nc.scalar.activation(w_hi[b % NHI][:, lo:lo + n], raw[b % NRAW][:, lo:lo + n], ACT.Copy) \
                        .then_inc(s_hi, 1)

            act.wait_ge(s_cols, 1)
            act.wait_ge(s_xT, 1)
            act.wait_ge(s_mean, 1)
            for k in range(KD):
                nc.scalar.activation(act_in[:, 0, k, :], bank[k // 2][:, (k % 2) * S:(k % 2 + 1) * S], ACT.Copy,
                                     scale=cols[:, ROW_G1 + k:ROW_G1 + k + 1]).then_inc(s_hTh, 1)
            split(0)
            split(1)
            for n in range(2):
                for t in range(T):
                    act.wait_ge(s_proj, 1 + 2 * n + t)
                    if n:
                        act.wait_ge(s_mean, 2)
                    nc.scalar.activation(squares[:, t], bank[2 * n + t][:], ACT.Square).then_inc(s_sumsq, 1)
                split(2 + n)
            act.wait_ge(s_bready, 1)
            for t in range(T):
                act.wait_ge(s_proj, 5 + t)
                nc.scalar.activation(vn[:, t], bank[4 + t][:], ACT.Copy).then_inc(s_vn, 1)
            split(4)

            for n, (name, j) in enumerate(UNITS):
                if n in SPLIT_AT:
                    split(SPLIT_AT[n])
                t = STEP.get(n, -1)
                if 0 <= t - 1 < PAIRS:
                    for h in (2 * (t - 1), 2 * (t - 1) + 1):
                        act.wait_ge(s_acc, h + 1)
                        if h >= 2:
                            act.wait_ge(s_o, h - 1)
                        nc.scalar.activation(attn_prob[:, h % 2], bank[head_bank(h)][:, 0:384], ACT.Exp) \
                            .then_inc(s_prob, 1)
                if 0 <= t < PAIRS:
                    for h in (2 * t, 2 * t + 1):
                        act.wait_ge(s_z, h + 1)
                        if h >= 2:
                            act.wait_ge(s_sp, h - 1)
                        nc.scalar.activation(soft[:, h % 2], bank[head_bank(h)][:, 0:384], ACT.Abs).then_inc(s_act, 1)
                        act.wait_ge(s_act, 2 * h + 1)
                        nc.scalar.activation(soft[:, h % 2], soft[:, h % 2], ACT.Exp, scale=-1.0).then_inc(s_act, 1)
                        act.wait_ge(s_act, 2 * h + 2)
                        nc.scalar.activation(soft[:, h % 2], soft[:, h % 2], ACT.Ln, bias=1.0).then_inc(s_ln, 1)
                if 0 <= t - 2 < PAIRS:
                    for h in (2 * (t - 2), 2 * (t - 2) + 1):
                        act.wait_ge(s_o, h + 1)
                        r = slice(h % 2 * HD, (h % 2 + 1) * HD)
                        nc.scalar.activation(mix_in[r, 1, 0, h // 2, :], bank[head_bank(h)][r, 0:S], ACT.Copy) \
                            .then_inc(s_oh, 1)
                if name == "mix":
                    act.wait_ge(s_unit, n + 1)
                    for g in (2 * j, 2 * j + 1):
                        nc.scalar.activation(mix_in[:, 0, 0, g, :], bank[6 + n % 2][:, (g % 2) * S:(g % 2 + 1) * S],
                                             ACT.Copy, scale=cols[:, ROW_PS + g:ROW_PS + g + 1]).then_inc(s_half, 1)
                if n == 8:
                    act.wait_ge(s_ev, 8)
                    nc.scalar.activation(gate_p.rearrange("p a b -> p (a b)"), gate_p.rearrange("p a b -> p (a b)"),
                                         ACT.Sigmoid).then_inc(s_sigp, 1)
                if name.startswith("ga"):
                    act.wait_ge(s_unit, n + 1)
                    k = 4 * int(name[2]) + 2 * j
                    nc.scalar.activation(gate_a[:, k:k + 2, :], bank[6 + n % 2][:].rearrange("p (a n) -> p a n", n=S),
                                         ACT.Sigmoid).then_inc(s_ga, 1)
                if name == "attn_up":
                    act.wait_ge(s_mf, j + 1)
                    nc.scalar.activation(act_in[:, 0, 2 * j:2 * j + 2, :], gate_p[:, 2 * j:2 * j + 2, :], ACT.Copy) \
                        .then_inc(s_mhi, 1)
            split(11)

            for t in range(T):
                act.wait_ge(s_x1, t + 1)
                nc.scalar.activation(gate_p.rearrange("p a b -> p (a b)")[:, t * D:(t + 1) * D], x1[:, t], ACT.Square,
                                     accum_out=tiny[:, t:t + 1]) \
                    .then_inc(s_sumsq, 1)
            act.wait_ge(s_hnT, 1)
            for b in (1, 3):
                for k in (2 * b, 2 * b + 1):
                    nc.scalar.activation(hT[:, k, :], bank[4 + b][:, (k % 2) * S:(k % 2 + 1) * S], ACT.Copy,
                                         scale=cols[:, ROW_G2 + k:ROW_G2 + k + 1]).then_inc(s_hT3, 1)
            act.wait_ge(s_rstd, 4)
            for t in range(T):
                nc.scalar.activation(parts[:, t, 0:D], x1[:, t], ACT.Copy, scale=tiny[:, 4 + t:5 + t]) \
                    .then_inc(s_p1, 1)
            for t in range(T):
                act.wait_ge(s_rest, t + 1)
                nc.scalar.activation(parts[:, t, D:2 * D], rest[:, t], ACT.Copy).then_inc(s_p1, 1)
            act.wait_ge(s_soft, 1)
            nc.scalar.activation(r_p, r_p, ACT.Exp).then_inc(s_softe, 1)

            act.wait_ge(s_table, 1)
            pairs = act.value_load(item_table[0:1, COLS:COLS + 1], min_val=E // 2, max_val=ITEMS // 2)
            with act.Fori(0, pairs) as i:
                for half in range(2):
                    act.wait_ge(s_glu, 2 * i + (half + 1))
                    nc.scalar.activation(sig, glu, ACT.Sigmoid, scale=ALPHA).then_inc(s_sig, 1)
                    if half == 0:
                        act.wait_ge(s_ptp, i + 1)
                        act.wait_ge(s_comb, i + 1)
                        nc.scalar.activation(place_T.rearrange("p a b -> p (a b)"), y_b[:, 0:T * P], ACT.Copy) \
                            .then_inc(s_pt, 1)
                    act.wait_ge(s_du, (2 * i + (half + 1)) * NDOWN)
                    for c in range(2):
                        last = nc.scalar.activation(y_pair[half * SLOTS:(half + 1) * SLOTS, c * FH:(c + 1) * FH],
                                                    y_b[c * SLOTS:(c + 1) * SLOTS, :], ACT.Copy)
                    last.then_inc(s_y, 1)
            for t in range(T):
                act.wait_ge(s_final, 2 * t + 2)
                nc.scalar.activation(gate_ring[:, 2 * t + 1, 0:FH], acc[2 * t + 1][:], ACT.Copy).then_inc(s_outa, 1)

        @block.vector
        def _(dve):
            order = [0]

            def link(ins):
                order[0] += 1
                ins.then_inc(s_dve, 1)
                dve.wait_ge(s_dve, order[0])

            def tt(o, a, b, op):
                return nc.vector.tensor_tensor(o, a, b, op)

            def mean(n, view, width):
                nc.vector.tensor_scalar(view[0], view[1], 1.0 / width, EPS, ALU.mult, ALU.add).then_inc(s_mean, 1)

            for g, w in enumerate(WINDOWS):
                for t in range(PAD):
                    if t < w:
                        nc.vector.memset(inv_count[:, g, t:t + 1], 1.0 / (t + 1))
                if w < PAD:
                    nc.vector.memset(inv_count[:, g, w:PAD], 1.0 / w)
            link(nc.vector.memset(tiny[:, 63:64], 0.0))
            dve.wait_ge(s_sumsq, 1)
            mean(0, (tiny[:, 2:4], tiny[:, 0:2]), D)
            dve.wait_ge(s_rstd, 1)
            for t in range(T):
                nc.vector.tensor_scalar(xn[:, t], x_sb[:, t], tiny[:, 4 + t:5 + t], None, ALU.mult) \
                    .then_inc(s_xn, 1)
            dve.wait_ge(s_rows, 1)
            nc.vector.tensor_copy(cols[:, 0:NROWS], bank[4][:, 0:NROWS]).then_inc(s_cols, 1)
            dve.wait_ge(s_cols, 1)

            def split(b):
                for lo, n, number in pieces(b):
                    dve.wait_ge(s_hi, number)
                    tt(w_lo[b % NRAW][:, lo:lo + n], raw[b % NRAW][:, lo:lo + n], w_hi_f[b % NHI][:, lo:lo + n],
                       ALU.subtract).then_inc(s_lo, 1)

            for k in range(KD):
                dve.wait_ge(s_hTh, k // 2 * 2 + 2)
                nc.vector.scalar_tensor_tensor(out=act_in[:, 1, k, :], in0=bank[k // 2][:, (k % 2) * S:(k % 2 + 1) * S],
                                               scalar=cols[:, ROW_G1 + k:ROW_G1 + k + 1],
                                               in1=act_f[:, 0, k * S:(k + 1) * S], op0=ALU.mult,
                                               op1=ALU.subtract).then_inc(s_hT, 1)
            split(0)
            split(1)
            dve.wait_ge(s_bias, 32)
            for stage, dst in ((stage_up, bias_up), (stage_down, bias_down)):
                mid = mid_part[:, 0:stage.shape[1]]
                link(nc.vector.tensor_copy(dst[0:E, :], stage))
                link(tt(stage, stage, dst[0:E, :], ALU.subtract))
                link(nc.vector.tensor_copy(mid, stage))
                link(nc.vector.tensor_copy(dst[E:2 * E, :], mid))
                link(tt(stage, stage, mid, ALU.subtract))
                link(nc.vector.tensor_copy(dst[2 * E:3 * E, :], stage))
            nc.vector.memset(tiny[:, 63:64], 0.0).then_inc(s_bready, 1)

            for n, dst in enumerate((qn, kn)):
                v = tiny[:, 16 + 16 * n:32 + 16 * n]
                for t in range(T):
                    dve.wait_ge(s_sumsq, 2 + 2 * n + t)
                    link(nc.vector.tensor_reduce(v[:, t * HEADS:(t + 1) * HEADS],
                                                 squares[:, t].rearrange("p (h d) -> p h d", d=HD), AX_X, ALU.add))
                mean(1 + n, (v, v), HD)
                dve.wait_ge(s_rstd, 2 + n)
                for t in range(T):
                    tt(dst[:, t].rearrange("p (h d) -> p h d", d=HD),
                       bank[2 * n + t][:].rearrange("p (h d) -> p h d", d=HD),
                       v[:, t * HEADS:(t + 1) * HEADS].unsqueeze(2).to_broadcast([P, HEADS, HD]), ALU.mult) \
                        .then_inc(s_qkn, 1)
                split(2 + n)
            for b in range(2):
                dve.wait_ge(s_tr, 1)
                nc.vector.tensor_scalar(qT[:, 2 * b:2 * b + 2, :], bank[6 + b][:].rearrange("p (a n) -> p a n", n=S),
                                        cols[:, ROW_Q:ROW_Q + 1], float(HD) ** -0.5, ALU.mult, ALU.mult) \
                    .then_inc(s_qk, 1)
            dve.wait_ge(s_tr, 2)
            dve.wait_ge(s_kz0, 1)
            kz_v = kz.rearrange("p (a h) n -> p a h n", h=2)
            for b in range(2):
                for half in range(2):
                    r = slice(half * HD, (half + 1) * HD)
                    nc.vector.tensor_scalar(kz_v[r, 2 * b:2 * b + 2, half, :],
                                            bank[b][r, :].rearrange("p (a n) -> p a n", n=S),
                                            cols[r, ROW_K:ROW_K + 1], None, ALU.mult).then_inc(s_qk, 1)
            split(4)
            for v in (uT, sumA, sumB):
                link(nc.vector.memset(v[:, :, 0:PAD], 0.0))

            for n, (name, j) in enumerate(UNITS):
                if n in SPLIT_AT:
                    split(SPLIT_AT[n])
                t = STEP.get(n, -1)
                if 0 <= t < PAIRS:
                    for h in (2 * t, 2 * t + 1):
                        dve.wait_ge(s_ln, h + 1)
                        if h >= 2:
                            dve.wait_ge(s_acc, h - 1)
                        nc.vector.scalar_tensor_tensor(out=spos[:, h % 2], in0=bank[head_bank(h)][:, 0:384],
                                                       scalar=0.0, in1=soft[:, h % 2], op0=ALU.max,
                                                       op1=ALU.add).then_inc(s_sp, 1)
                if 0 <= t - 2 < PAIRS:
                    for h in (2 * (t - 2), 2 * (t - 2) + 1):
                        dve.wait_ge(s_oh, h + 1)
                        r = slice(h % 2 * HD, (h % 2 + 1) * HD)
                        tt(mix_in[r, 1, 1, h // 2, :], bank[head_bank(h)][r, 0:S],
                           mix_f[r, 2, h // 2 * S:(h // 2 + 1) * S], ALU.subtract).then_inc(s_oT, 1)
                both = bank[6 + n % 2][:].rearrange("p (a n) -> p a n", n=S)
                if name == "u":
                    dve.wait_ge(s_unit, n + 1)
                    nc.vector.tensor_copy(uT[:, 2 * j:2 * j + 2, PAD:], both).then_inc(s_ev, 1)
                    if j == 1:
                        dve.wait_ge(s_ev, n + 1)
                        src = uT
                        for level in range(G):
                            dst = (sumA, sumB)[level % 2]
                            step = 1 << level
                            link(tt(dst[:, level:, PAD:], src[:, level:, PAD:], src[:, level:, PAD - step:UW - step],
                                    ALU.add))
                            src = dst
                        for g, w in enumerate(WINDOWS):
                            s = (sumA, sumB)[g % 2][:, g]
                            link(tt(s[:, 0:PAD], s[:, PAD:2 * PAD], inv_count[:, g, :], ALU.mult))
                            nc.vector.scalar_tensor_tensor(out=uT[:, g, 2 * PAD:], in0=s[:, 2 * PAD:], scalar=1.0 / w,
                                                           in1=uT[:, g, 2 * PAD:], op0=ALU.mult, op1=ALU.subtract)
                            link(tt(uT[:, g, PAD:2 * PAD], s[:, 0:PAD], uT[:, g, PAD:2 * PAD], ALU.subtract))
                        nc.vector.memset(tiny[:, 63:64], 0.0).then_inc(s_dT, 1)
                elif name.startswith("gp"):
                    dve.wait_ge(s_unit, n + 1)
                    k = 4 * int(name[2]) + 2 * j
                    nc.vector.tensor_copy(gate_p[:, k:k + 2, :], both).then_inc(s_ev, 1)
                elif name == "mix":
                    for g in (2 * j, 2 * j + 1):
                        dve.wait_ge(s_half, 2 * j + 2)
                        last = nc.vector.scalar_tensor_tensor(
                            out=mix_in[:, 0, 1, g, :], in0=both[:, g % 2], scalar=cols[:, ROW_PS + g:ROW_PS + g + 1],
                            in1=mix_f[:, 0, g * S:(g + 1) * S], op0=ALU.mult, op1=ALU.subtract)
                    last.then_inc(s_ev, 1)
                elif name == "pool_up":
                    dve.wait_ge(s_sigp, 1)
                    dve.wait_ge(s_unit, n + 1)
                    v = gate_p[:, 2 * j:2 * j + 2, :]
                    tt(v, both, v, ALU.mult).then_inc(s_ev, 1)
                elif name == "attn_up":
                    dve.wait_ge(s_unit, n + 1)
                    dve.wait_ge(s_ga, 4)
                    v, m = gate_a[:, 2 * j:2 * j + 2, :], gate_p[:, 2 * j:2 * j + 2, :]
                    tt(v, both, v, ALU.mult).then_inc(s_ev, 1)
                    dve.wait_ge(s_ev, n - 3)
                    tt(m, m, v, ALU.add).then_inc(s_mf, 1)
                    dve.wait_ge(s_mhi, j + 1)
                    dve.wait_ge(s_mf, j + 1)
                    tt(act_in[:, 1, 2 * j:2 * j + 2, :], m, carve(act_f[:, 0, :], 2 * j * S, 2, S), ALU.subtract) \
                        .then_inc(s_mrg, 1)
            split(11)

            for n in range(2):
                for t in range(T):
                    dve.wait_ge(s_wo, 2 * n + t + 1)
                    last = tt(x1[:, t, n * FH:(n + 1) * FH], acc[2 * t + n][:], x_sb[:, t, n * FH:(n + 1) * FH],
                              ALU.add)
                    if n == 1:
                        last.then_inc(s_x1, 1)
            dve.wait_ge(s_sumsq, 7)
            mean(3, (tiny[:, 2:4], tiny[:, 0:2]), D)
            dve.wait_ge(s_hnT, 1)
            for b in (0, 2):
                tt(hT[:, 2 * b:2 * b + 2, :], bank[4 + b][:].rearrange("p (a n) -> p a n", n=S),
                   cols[:, ROW_G2 + 2 * b:ROW_G2 + 2 * b + 2].unsqueeze(2).to_broadcast([P, 2, S]), ALU.mult) \
                    .then_inc(s_hT2, 1)
            dve.wait_ge(s_rstd, 4)
            for t in range(T):
                nc.vector.tensor_scalar(rest[:, t], x1[:, t], tiny[:, 4 + t:5 + t], None, ALU.mult).then_inc(s_hn, 1)
            for t in range(T):
                dve.wait_ge(s_hn, t + 1)
                dve.wait_ge(s_p1, t + 1)
                tt(rest[:, t], rest[:, t], parts[:, t, 0:D], ALU.subtract).then_inc(s_rest, 1)
            dve.wait_ge(s_lgT, 1)
            nc.vector.tensor_copy(lgT, bank[4][0:E, 0:S]).then_inc(s_lgTs, 1)
            dve.wait_ge(s_lg, 1)
            for t in range(T):
                last = nc.vector.scalar_tensor_tensor(out=r_lg[:, t], in0=bank[5][:, t * E:(t + 1) * E],
                                                      scalar=tiny[:, 4 + t:5 + t], in1=router_b[:], op0=ALU.mult,
                                                      op1=ALU.add)
            link(last)
            for t in range(T):
                link(nc.vector.max(r_top[:, t], r_lg[:, t]))
            for t in range(T):
                last = nc.vector.max_index(r_idx[:, t], r_top[:, t], r_lg[:, t])
            link(last)
            tt(r_p, r_top, r_top[:, :, 0:1].to_broadcast([P, T, 8]), ALU.subtract).then_inc(s_soft, 1)
            link(nc.vector.tensor_copy(r_idf, r_idx))
            dve.wait_ge(s_const, N_CONST)
            eq4 = r_eq.rearrange("p (t r) e -> p t r e", r=TOP_K)
            eqp4 = r_eqp.rearrange("p (t r) e -> p t r e", r=TOP_K)
            for t in range(T):
                last = tt(eq4[:, t], r_iota.unsqueeze(1).to_broadcast([P, TOP_K, E]),
                          r_idf[:, t, 0:TOP_K].unsqueeze(2).to_broadcast([P, TOP_K, E]), ALU.is_equal)
            link(last)
            with nc.allow_low_precision(reason="sums of four zeros and ones, at most one of them a one"):
                nc.vector.tensor_reduce(r_sel, eq4.rearrange("p t r e -> p t e r"), AX_X, ALU.add).then_inc(s_sel, 1)
            dve.wait_ge(s_softe, 1)
            link(nc.vector.tensor_reduce(r_s[:, 0:T], r_p[:, :, 0:TOP_K], AX_X, ALU.add))
            link(nc.vector.reciprocal(r_s[:, 0:T], r_s[:, 0:T]))
            link(tt(r_p, r_p, r_s[:, 0:T].unsqueeze(2).to_broadcast([P, T, 8]), ALU.mult))
            for t in range(T):
                last = tt(eqp4[:, t], eq4[:, t], r_p[:, t, 0:TOP_K].unsqueeze(2).to_broadcast([P, TOP_K, E]), ALU.mult)
            link(last)
            link(nc.vector.tensor_reduce(gate_item[:, :, 0:E], eqp4.rearrange("p t r e -> p t e r"), AX_X, ALU.add))
            dve.wait_ge(s_cnt, 1)
            link(nc.vector.scalar_tensor_tensor(out=r_pos, in0=bank[6][:, 0:T * E].rearrange("p (t e) -> p t e", e=E),
                                                scalar=FAR, in1=r_sel, op0=ALU.add, op1=ALU.mult))
            nc.vector.memset(pos_item[:, :, ITEMS:], -FAR)
            nc.vector.memset(gate_item[:, :, ITEMS:], 0.0)
            link(nc.vector.tensor_scalar(pos_item[:, :, 0:E], r_pos, FAR, None, ALU.subtract))

            def places(at):
                iota4 = iota64[:].unsqueeze(1).to_broadcast([P, 2, SLOTS])
                for t in range(T):
                    tt(place_bf[:, t].rearrange("p (j s) -> p j s", s=SLOTS), iota4,
                       pos_item[:, t, at].unsqueeze(2).to_broadcast([P, 2, SLOTS]), ALU.is_equal) \
                        .then_inc(s_onehot, 1)
                return at

            def gated(at):
                for t in range(T):
                    last = tt(place_g[:, t].rearrange("p (j s) -> p j s", s=SLOTS),
                              place_bf[:, t].rearrange("p (j s) -> p j s", s=SLOTS),
                              gate_item[:, t, at].unsqueeze(2).to_broadcast([P, 2, SLOTS]), ALU.mult)
                last.then_inc(s_place, 1)

            def selector(half, col, signal):
                nc.vector.tensor_copy(sel_item[:, half, :], item_sel[:, col].to_broadcast([3 * E, SLOTS])) \
                    .then_inc(signal, 1)

            def evacuate_gather(r):
                src = (t_b, y_b)[r][:].rearrange("p (a n) -> p a n", n=P)
                g = cols[:, ROW_G2 + 4 * r:ROW_G2 + 4 * r + 4].unsqueeze(2).to_broadcast([P, 4, P])
                tt(hT_items[:, 4 * r:4 * r + 4, :], src, g, ALU.mult).then_inc(s_gev, 1)

            places(slice(0, 2))
            dve.wait_ge(s_onehot, T)
            gated(slice(0, 2))
            selector(0, slice(0, 1), s_sela)

            cnt = lin_b[0:E, 0:MAX_OVER]
            dve.wait_ge(s_tab, 1)
            link(nc.vector.tensor_scalar(o_cnt, cnt, float(SLOTS), None, ALU.is_gt))
            for m in (2, 3):
                link(nc.vector.scalar_tensor_tensor(out=o_cnt, in0=cnt, scalar=float(m * SLOTS), in1=o_cnt,
                                                    op0=ALU.is_gt, op1=ALU.add))
            nc.vector.tensor_copy(o_cbf, o_cnt).then_inc(s_tabv, 1)
            dve.wait_ge(s_gps, 1)
            evacuate_gather(0)
            dve.wait_ge(s_tab, 2)
            link(nc.vector.tensor_scalar(o_row[:, 0:1], lin_b[0:1, 128:129], -1.0, None, ALU.mult))
            link(nc.vector.tensor_scalar(o_row[:, 2:2 + MAX_OVER // 2],
                                         o_j[0:1, :].rearrange("p (a b) -> p b a", b=2)[:, 0, :],
                                         o_row[:, 0:1], None, ALU.is_lt))
            link(nc.vector.tensor_reduce(o_row[:, 1:2], o_row[:, 2:2 + MAX_OVER // 2], AX_X, ALU.add))
            nc.vector.tensor_scalar(item_table[0:1, COLS:COLS + 1], o_row[:, 1:2], 1.0, float(E // 2),
                                    ALU.mult, ALU.add).then_inc(s_table, 1)
            nc.vector.tensor_copy(o_T, glu_b[0:E, :].rearrange("p (a n) -> p a n", n=P))
            link(tt(o_a, o_j, lin_b[0:E, 64:64 + MAX_OVER], ALU.subtract))
            link(tt(o_b, o_a, o_cnt, ALU.is_lt))
            link(nc.vector.scalar_tensor_tensor(out=o_sel[:, 0], in0=o_a, scalar=0.0, in1=o_b, op0=ALU.is_ge,
                                                op1=ALU.mult))
            link(nc.vector.scalar_tensor_tensor(out=o_blk, in0=o_a, scalar=1.0, in1=o_sel[:, 0], op0=ALU.add,
                                                op1=ALU.mult))
            link(nc.vector.tensor_scalar(o_blk, o_blk, float(SLOTS), None, ALU.mult))
            nc.vector.tensor_scalar(o_sel[:, 1], o_sel[:, 0], o_e[:, 0:1], None, ALU.mult).then_inc(s_tabv, 1)
            dve.wait_ge(s_gps, 2)
            evacuate_gather(1)
            for part in range(3):
                nc.vector.tensor_copy(item_sel[part * E:(part + 1) * E, E:ITEMS], o_sel[:, 0])
            dve.wait_ge(s_tab, 3)
            nc.vector.tensor_scalar(pos_item[:, :, E:ITEMS], glu_b[:, 0:T * MAX_OVER]
                                    .rearrange("p (t j) -> p t j", t=T), FAR, None, ALU.subtract)
            nc.vector.tensor_copy(gate_item[:, :, E:ITEMS], glu_b[:, T * MAX_OVER:2 * T * MAX_OVER]
                                  .rearrange("p (t j) -> p t j", t=T))
            row = lin_b[0:1, 192:192 + MAX_OVER]
            nc.vector.tensor_scalar(item_table[0:1, E:ITEMS], row, -1.0, None, ALU.mult).then_inc(s_ids, 1)
            nc.vector.memset(tiny[:, 63:64], 0.0).then_inc(s_sr, 1)

            dve.wait_ge(s_table, 1)
            pairs = dve.value_load(item_table[0:1, COLS:COLS + 1], min_val=E // 2, max_val=ITEMS // 2)
            with dve.Fori(0, pairs) as i:
                for half in range(2):
                    n1 = 2 * i + (half + 1)
                    dve.wait_ge(s_gu, n1 * KD)
                    nc.vector.tensor_scalar(glu, glu_b[:], LIMIT, None, ALU.min).then_inc(s_glu, 1)
                    nc.vector.tensor_scalar(lin, lin_b[:], LIMIT, -LIMIT, ALU.min, ALU.max).then_inc(s_sr, 1)
                    dve.wait_ge(s_glu, n1)
                    dve.wait_ge(s_sr, n1 + 1)
                    nc.vector.scalar_tensor_tensor(out=lin, in0=lin, scalar=1.0, in1=glu, op0=ALU.add,
                                                   op1=ALU.mult).then_inc(s_dve2, 1)
                    if half == 1:
                        dve.wait_ge(s_gps, 2 * i + 3)
                        evacuate_gather(0)
                    dve.wait_ge(s_dve2, n1)
                    dve.wait_ge(s_sig, n1)
                    tt(lin, lin, sig, ALU.mult).then_inc(s_actr, 1)
                    if half == 1:
                        dve.wait_ge(s_gps, 2 * i + 4)
                        evacuate_gather(1)
                    dve.wait_ge(s_aps, n1)
                    nc.vector.tensor_copy(actT, t_b[:].rearrange("p (a n) -> p a n", n=P)).then_inc(s_actT, 1)
                    if half == 0:
                        selector(1, bass.ds(2 * i + 1, 1), s_selb)
                        dve.wait_ge(s_ptp, i + 1)
                        ahead = bass.ds(2 * i + 2, 2)
                        places(ahead)
                        dve.wait_ge(s_onehot, T * i + 2 * T)
                        gated(ahead)
                    else:
                        selector(0, bass.ds(2 * i + 2, 1), s_sela)
            for t in range(T):
                dve.wait_ge(s_final, 2 * t + 1)
                nc.vector.tensor_copy(gate_ring[:, 2 * t, 0:FH], acc[2 * t][:]).then_inc(s_outv, 1)

        @block.tensor
        def _(pe):
            def mm(o, lhsT, rhs, start):
                return nc.tensor.matmul(o, lhsT, rhs, start=start, stop=True, skip_group_check=True)

            pe.wait_ge(s_const, 1)
            pe.wait_ge(s_rw, 16 * 7)
            nc.tensor.transpose(bank[4][:, 0:NROWS], rows[0:NROWS], ident[0:NROWS, 0:NROWS]).then_inc(s_rows, 1)
            pe.wait_ge(s_xn, T)
            for k in range(KD):
                for t in range(T):
                    last = nc.tensor.transpose(bank[k // 2][:, (k % 2) * S + t * P:(k % 2) * S + (t + 1) * P],
                                               xn[:, t, k * P:(k + 1) * P], ident[:])
            last.then_inc(s_xT, 1)

            def mm3(o, stat, mov, start):
                mm(o, stat[0], mov[0], start)
                mm(o, stat[0], mov[1], False)
                return mm(o, stat[1], mov[0], False)

            def weights(b, k, width, cols_at, n):
                at = k * width + cols_at
                return w_hi[b % NHI][:, at:at + n], w_lo[b % NRAW][:, at:at + n]

            def acts(k, cols_at=0, n=S):
                return act_in[:, 0, k, cols_at:cols_at + n], act_in[:, 1, k, cols_at:cols_at + n]

            def wait_split(b, k, width):
                for lo, _, number in pieces(b):
                    if lo == k * width:
                        pe.wait_ge(s_lo, number)

            def project(b, name):
                for t in range(T):
                    for k in range(KD):
                        if t == 0:
                            wait_split(b, k, BLK)
                            if b == 0:
                                pe.wait_ge(s_hT, k + 1)
                        last = mm3(bank[2 * b + t][:], acts(k, t * P, P), weights(b, k, BLK, 0, BLK), k == 0)
                    last.then_inc(s_proj, 1)

            def transposed(src, b, count):
                pe.wait_ge(s_qkn, count)
                for a in range(PAIRS):
                    for t in range(T):
                        last = nc.tensor.transpose(
                            bank[b + a // 2][:, (a % 2) * S + t * P:(a % 2) * S + (t + 1) * P],
                            src[:, t, a * P:(a + 1) * P], ident[:])
                last.then_inc(s_tr, 1)

            project(0, "q")
            project(1, "k")
            transposed(qn, 6, T)
            project(2, "v")
            transposed(kn, 0, 2 * T)

            pe.wait_ge(s_const, 7)
            pe.wait_ge(s_qk, 6)
            pe.wait_ge(s_vn, T)
            for n, (name, j) in enumerate(UNITS):
                t = STEP.get(n, -1)
                if 0 <= t - 2 < PAIRS:
                    for h in (2 * (t - 2), 2 * (t - 2) + 1):
                        pe.wait_ge(s_prob, h + 1)
                        half = h % 2
                        o = bank[head_bank(h)][half * HD:(half + 1) * HD, :]
                        mm(o[:, 0:S], vn[:, 0, h * HD:(h + 1) * HD], attn_prob[:, half, 0:S], True)
                        mm(o[:, P:S], vn[:, 1, h * HD:(h + 1) * HD], attn_prob[:, half, S:S + P], False) \
                            .then_inc(s_o, 1)
                if 0 <= t - 1 < PAIRS:
                    for h in (2 * (t - 1), 2 * (t - 1) + 1):
                        pe.wait_ge(s_sp, h + 1)
                        o, s = bank[head_bank(h)], spos[:, h % 2]
                        mm(o[:, 0:S + P], from_key, s, False)
                        mm(o[:, P:S], minus, s[:, S:S + P], False).then_inc(s_acc, 1)
                if 0 <= t < PAIRS:
                    if t >= 3:
                        pe.wait_ge(s_oT, 2 * (t - 3) + 2)
                    for h in (2 * t, 2 * t + 1):
                        o = bank[head_bank(h)]
                        mm(o[:, 0:S], kz[:, h, 0:P], qT[:, h // 2, :], True)
                        mm(o[:, S:S + P], kz[:, h, P:S], qT[:, h // 2, P:S], False)
                        mm(o[:, 0:P], ident_bf, mask_bf, False)
                        mm(o[:, S:S + P], ident_bf, mask_bf, False).then_inc(s_z, 1)
                if n >= 2:
                    unit_wait(pe, n - 2)
                o = bank[6 + n % 2]
                for half in range(2):
                    dst = o[:, half * S:(half + 1) * S]
                    if name == "mix":
                        if n == 4 and half == 0:
                            pe.wait_ge(s_dT, 1)
                            pe.wait_ge(s_small, 16 * 3)
                        last = mm(dst, grp_w[:, 2 * j + half, :], uT[:, 2 * j + half, PAD:], half == 0)
                        continue
                    b = BLOCKS.index(name)
                    if name in ("pool_up", "attn_up"):
                        which = name == "attn_up"
                        if j == 0 and half == 0:
                            pe.wait_ge(s_oT, HEADS) if which else unit_wait(pe, 5)
                        for k in range(G):
                            if j == 0 and half == 0:
                                wait_split(b, k, D)
                            last = mm3(dst, weights(b, k, D, (2 * j + half) * P, P),
                                       (mix_in[:, int(which), 0, k, :], mix_in[:, int(which), 1, k, :]),
                                       half == 0 and k == 0)
                        continue
                    for k in range(KD):
                        if j == 0 and half == 0:
                            wait_split(b, k, BLK)
                        last = mm3(dst, weights(b, k, BLK, (2 * j + half) * P, P), acts(k), half == 0 and k == 0)
                last.then_inc(s_unit, 1)
            for n in range(2):
                b = BLOCKS.index(f"out{n}")
                for t in range(T):
                    for k in range(KD):
                        if t == 0:
                            wait_split(b, k, BLK)
                            if n == 0 and k % 2 == 0:
                                pe.wait_ge(s_mrg, k // 2 + 1)
                        last = mm3(acc[2 * t + n][:], acts(k, t * P, P), weights(b, k, BLK, 0, BLK), k == 0)
                    last.then_inc(s_wo, 1)
            for t in range(T):
                pe.wait_ge(s_x1, t + 1)
                for k in range(KD):
                    last = nc.tensor.transpose(bank[4 + k // 2][:, (k % 2) * S + t * P:(k % 2) * S + (t + 1) * P],
                                               x1[:, t, k * P:(k + 1) * P], ident[:])
            last.then_inc(s_hnT, 1)
            for k in range(KD):
                if k == 0:
                    pe.wait_ge(s_hT2, 2)
                    pe.wait_ge(s_hT3, 1)
                if k % 2 == 0 and k:
                    pe.wait_ge((s_hT2, s_hT3)[k // 2 % 2], (2, 2, 2, 4)[k // 2])
                last = mm(bank[4][0:E, 0:S], router_w[:, k, :], hT[:, k, :], k == 0)
            last.then_inc(s_lgT, 1)
            pe.wait_ge(s_lgTs, 1)
            for t in range(T):
                last = nc.tensor.transpose(bank[5][:, t * E:(t + 1) * E], lgT[:, t * P:(t + 1) * P], ident[0:E, 0:E])
            last.then_inc(s_lg, 1)
            pe.wait_ge(s_x1, T)
            for t in range(T):
                for n in range(2):
                    mm(acc[2 * t + n][:], ident[:], x_sb[:, t, n * FH:(n + 1) * FH], False)
            pe.wait_ge(s_sel, 1)
            mm(bank[6][:, 0:E], below_bf[:], r_sel[:, 0], True)
            mm(bank[6][:, E:2 * E], ones_bf[:], r_sel[:, 0], False)
            mm(bank[6][:, E:2 * E], below_bf[:], r_sel[:, 1], False).then_inc(s_cnt, 1)
            for t in range(T):
                last = mm(lin_b[0:E, 0:MAX_OVER], r_sel[:, t], ones_bf[:, 0:MAX_OVER], t == 0)
            last.then_inc(s_tab, 1)

            def gather(r):
                o = (t_b, y_b)[r]
                for k in range(4 * r, 4 * r + 4):
                    for t in range(T):
                        for part in range(3):
                            last = mm(o[:, (k % 4) * P:(k % 4 + 1) * P],
                                      parts[:, t, part * D + k * P:part * D + (k + 1) * P], place_bf[:, t, :],
                                      k == 4 * r and t == 0 and part == 0)
                last.then_inc(s_gps, 1)

            pe.wait_ge(s_parts, T)
            pe.wait_ge(s_place, 1)
            gather(0)
            for t in range(T):
                nc.tensor.transpose(glu_b[0:E, t * P:(t + 1) * P], r_pos[:, t], ident[:])
                nc.tensor.transpose(glu_b[0:E, (T + t) * P:(T + t + 1) * P], gate_item[:, t, 0:E], ident[:])
            pe.wait_ge(s_tabv, 1)
            pe.wait_ge(s_const, N_CONST)
            mm(lin_b[0:1, 128:129], o_neg[:, 0:1], o_cnt[:, 0:1], True)
            mm(lin_b[0:E, 64:64 + MAX_OVER], below_bf[0:E, 0:E], o_cbf, False).then_inc(s_tab, 1)
            gather(1)
            pe.wait_ge(s_tabv, 2)
            for t in range(T):
                v = glu_b[:, t * MAX_OVER:(t + 1) * MAX_OVER]
                mm(v, o_T[:, t, :], o_sel[:, 0], t == 0)
                mm(v, o_neg, o_blk, False)
                mm(glu_b[:, (T + t) * MAX_OVER:(T + t + 1) * MAX_OVER], o_T[:, T + t, :], o_sel[:, 0], False)
            mm(lin_b[0:1, 192:192 + MAX_OVER], o_neg[:, 0:1], o_sel[:, 1], True).then_inc(s_tab, 1)

            def combine():
                for t in range(T):
                    for n in range(2):
                        yield mm(acc[2 * t + n][:], place_T[:, t, :], y_pair[:, n * FH:(n + 1) * FH], False)

            pe.wait_ge(s_table, 1)
            pairs = pe.value_load(item_table[0:1, COLS:COLS + 1], min_val=E // 2, max_val=ITEMS // 2)
            with pe.Fori(0, pairs) as i:
                for half in range(2):
                    n0 = 2 * i + half
                    slots = slice(half * SLOTS, (half + 1) * SLOTS)
                    if half == 0:
                        pe.wait_ge(s_gev, 2 * i + 2)
                        pe.wait_ge(s_sela, i + 1)
                    else:
                        pe.wait_ge(s_selb, i + 1)
                    pe.wait_ge(s_sr, n0 + 1)
                    for c in range(2):
                        for b, m in ((glu_b, 0), (lin_b, 1)):
                            lo = m * D + c * FH
                            mm(b[c * SLOTS:(c + 1) * SLOTS, :], sel_item[:, half, :], bias_up[:, lo:lo + FH], True)
                    for k in range(KD):
                        s = SLOT[half][k]
                        pe.wait_ge(s_gl[s], 16 * i + 16)
                        for b, m in ((glu_b, 0), (lin_b, 1)):
                            for c in range(2):
                                lo = m * D + c * FH
                                last = mm(b[c * SLOTS:(c + 1) * SLOTS, :], hT_items[:, k, slots],
                                          gate_ring[:, s, lo:lo + FH], False)
                        last.then_inc(s_gu, 1)
                    if half == 0:
                        pe.wait_ge(s_y, 2 * i + 1)
                        for last in combine():
                            pass
                        last.then_inc(s_comb, 1)
                        pe.wait_ge(s_place, i + 1)
                        for t in range(T):
                            last = nc.tensor.transpose(y_b[:, t * P:(t + 1) * P], place_g[:, t], ident[:])
                        last.then_inc(s_ptp, 1)
                    else:
                        pe.wait_ge(s_place, i + 2)
                        gather(0)
                        pe.wait_ge(s_y, 2 * i + 2)
                        gather(1)
                        pe.wait_ge(s_gev, 2 * i + 3)
                    pe.wait_ge(s_actr, n0 + 1)
                    for c in range(FH // P):
                        last = nc.tensor.transpose(t_b[:, c * P:(c + 1) * P], lin[:, c * P:(c + 1) * P], ident[:])
                    last.then_inc(s_aps, 1)
                    if half == 0:
                        pe.wait_ge(s_pt, i + 1)
                    else:
                        pe.wait_ge(s_gev, 2 * i + 4)
                    for c in range(2):
                        mm(y_b[c * SLOTS:(c + 1) * SLOTS, :], sel_item[:, half, :], bias_down[:, c * FH:(c + 1) * FH],
                           True)
                    pe.wait_ge(s_actT, n0 + 1)
                    for k in range(KD):
                        if k % 2 == 0:
                            pe.wait_ge(s_dl[k // 2], 32 * i + 16 * (half + 1))
                        f0 = (k // 4) * SLOTS
                        for c in range(2):
                            last = mm(y_b[c * SLOTS:(c + 1) * SLOTS, :], actT[:, k % 4, f0:f0 + SLOTS],
                                      down_ring[:, k // 2, k % 2, c * FH:(c + 1) * FH], False)
                        if k % 2:
                            last.then_inc(s_du, 1)
            pe.wait_ge(s_y, 2 * pairs + 1)
            for last in combine():
                last.then_inc(s_final, 1)


_INS = ["x", "norm1_g", "w_in", "q_norm_g", "k_norm_g", "w_pool_grp", "pool_scale", "w_pool_up", "w_attn_up",
        "w_out", "norm2_g", "w_router", "b_router", "w_gate_up", "b_gate_up", "w_down", "b_down"]


def kernel(**inputs):
    import numpy as _np
    import concourse.bacc as _bacc
    from concourse import mybir as _mybir
    from concourse.bass_utils import run_bass_kernel_spmd as _run

    nc = _bacc.Bacc("TRN2", target_bir_lowering=False, num_devices=1)
    arrays, args = {}, []
    for name in _INS:
        a = _np.ascontiguousarray(inputs[name])
        arrays[f"in_{name}_dram"] = a
        args.append(nc.dram_tensor(f"in_{name}_dram", a.shape, _mybir.dt.from_np(a.dtype),
                                   kind="ExternalInput").ap())
    out = nc.dram_tensor("out_0_dram", inputs["x"].shape, _mybir.dt.float32, kind="ExternalOutput").ap()
    hybrid_block_kernel(nc, *args, out)
    r = _run(nc, [arrays], core_ids=[0])
    return r.results[0]["out_0_dram"]
```

```python
from contextlib import ExitStack

import concourse.bass as bass
from concourse import mybir

P = 128
ALU = mybir.AluOpType
ACT = mybir.ActivationFunctionType
F32 = mybir.dt.float32
F32R = mybir.dt.float32r
BF16 = mybir.dt.bfloat16
I32 = mybir.dt.int32
U32 = mybir.dt.uint32
AX_X = mybir.AxisListType.X

WINDOWS = (2, 4, 8, 16)
TOP_K = 4
LIMIT = 7.0
ALPHA = 1.702
EPS = 1e-6
FAR = 1000.0
MASKED = -1.0e30


def hybrid_block_kernel(nc, x, norm1_g, w_in, q_norm_g, k_norm_g, w_pool_grp, pool_scale, w_pool_up,
                        w_attn_up, w_out, norm2_g, w_router, b_router, w_gate_up, b_gate_up, w_down,
                        b_down, out):
    D = x.shape[2]
    S = x.shape[1]
    T = S // P
    KD = D // P
    E = w_router.shape[2]
    HD = q_norm_g.shape[1]
    HEADS = w_attn_up.shape[1] // HD
    PAIRS = HEADS // 2
    G = len(WINDOWS)
    BLK = 512
    FH = D // 2
    SLOTS = 64
    MAX_OVER = S * TOP_K // SLOTS
    ITEMS = E + MAX_OVER
    COLS = ITEMS + 2
    NSLOT = 2 * KD
    NDOWN = KD // 2
    PAD = max(WINDOWS)
    COLT = P // E
    EARLY = 5
    assert T == 2 and D == 1024 and HD == 64 and HEADS == 8 and G == 4 and E == 32

    x_t = x[0].rearrange("(t p) d -> p t d", p=P)
    out_t = out[0].rearrange("(t p) d -> t p d", p=P)
    w_in_b = w_in[0].rearrange("(k p) (b n) -> b p k n", p=P, n=BLK)

    with ExitStack() as ctx:
        def sb(name, shape, dt=F32):
            return ctx.enter_context(nc.sbuf_tensor(name, shape, dt))

        def sem(name):
            return ctx.enter_context(nc.semaphore(name))

        ring_at = (nc.sbuf_base + 31) // 32 * 32
        gate_ring = sb("gate_ring", [P, NSLOT, 2 * D])
        scratch_at = (nc.sbuf_base + 31) // 32 * 32
        down_ring = sb("down_ring", [P, NDOWN, 2, D])
        area_x = sb("area_x", [P, 2 * D])
        area_m = sb("area_m", [P, 7360])
        bias_up = sb("bias_up", [3 * E, 2 * D], BF16)
        bias_down = sb("bias_down", [3 * E, D], BF16)
        ident = sb("ident", [P, P])
        iota64 = sb("iota64", [P, SLOTS])
        ones_bf = sb("ones_bf", [P, P], BF16)
        below_bf = sb("below_bf", [P, P], BF16)
        cols = sb("cols", [P, 24])
        router_w = sb("router_w", [P, KD, E])
        router_b = sb("router_b", [P, E])
        tiny = sb("tiny", [P, 64])
        pos_item = sb("pos_item", [P, T, COLS])
        gate_item = sb("gate_item", [P, T, COLS])
        item_sel = sb("item_sel", [3 * E, COLS], BF16)
        sel_item = sb("sel_item", [3 * E, 2, SLOTS], BF16)
        item_table = sb("item_table", [1, COLS + 2], I32)

        def carve(area, lo, *dims, dt=F32):
            n = 1
            for d in dims:
                n *= d
            words = n if dt in (F32, I32, U32) else n // 2
            v = area[:, lo:lo + words]
            if dt != F32:
                v = v.bitcast(dt)
            if len(dims) == 2:
                v = v.rearrange("p (a b) -> p a b", b=dims[1])
            if len(dims) == 3:
                v = v.rearrange("p (a b c) -> p a b c", b=dims[1], c=dims[2])
            return v

        NRAW, NHI, BW = 5, 2, KD * BLK
        HW = BW // 2
        HI_AT, PR_AT = 6, 5

        def buffer(name, at, dt):
            return nc.alloc_sbuf_tensor_at(name, [P, BW], dt, offset=ring_at + at * BW * 4)

        raw = [buffer(f"raw{j}", j, F32) for j in range(NRAW)]
        w_lo = [buffer(f"w_lo{j}", j, F32R) for j in range(NRAW)]
        w_hi = [buffer(f"w_hi{j}", HI_AT + j, F32R) for j in range(NHI)]
        mix_in = nc.alloc_sbuf_tensor_at("mix_in", [P, 2, 2, PAIRS, S], F32R, offset=ring_at + PR_AT * BW * 4)
        act_in = nc.alloc_sbuf_tensor_at("act_in", [P, 2, KD, S], F32R, offset=scratch_at)
        w_hi_f = [w[:].bitcast(F32) for w in w_hi]
        mix_f = mix_in[:].rearrange("p a b c n -> p (a b) (c n)").bitcast(F32)

        scratch = down_ring[:].rearrange("p a b c -> p (a b c)")
        x_sb = carve(area_x, 0, T, D)
        act_f = act_in[:].rearrange("p a k n -> p a (k n)").bitcast(F32)
        hT = carve(scratch, 0, KD, S)
        kz = carve(scratch, 4096, HEADS, S)
        xn = carve(scratch, 4096, T, D)
        x1 = carve(scratch, 4096, T, D)
        squares = carve(scratch, 6144, 2, BLK)
        soft = carve(scratch, 6144, 2, 384)
        spos = carve(scratch, 6912, 2, 384)
        stage_down = carve(scratch, 6144, D)[0:E]
        rest = carve(scratch, 2048, T, D)
        UW = PAD + S
        uT = carve(area_m, 0, G, UW)
        rows = carve(area_m, 0, P)
        mid_part = carve(area_m, 0, 2 * D, dt=BF16)[0:E]
        qn = carve(area_m, 1088, T, BLK)
        kn = carve(area_m, 2176, T, BLK)
        sumA = carve(area_m, 1088, G, UW)
        sumB = carve(area_m, 2176, G, UW)
        gate_p = carve(area_m, 1088, KD, S)
        vn = carve(area_m, 3264, T, BLK)
        qT = carve(area_m, 4288, PAIRS, S)
        stage_up = carve(area_m, 3264, 2 * D)[0:E]
        attn_prob = carve(area_m, 5312, 2, 384)
        gate_a = carve(area_m, 5312, KD, S)
        grp_w = carve(area_m, 6336, G, P)
        from_key = carve(area_m, 6848, P)
        minus = carve(area_m, 6976, P)
        ident_bf = carve(area_m, 7104, P, dt=BF16)
        mask_bf = carve(area_m, 7168, P, dt=BF16)
        inv_count = carve(area_m, 7232, G, PAD)
        parts = carve(area_m, 0, T, 3 * D, dt=BF16)
        hT_items = carve(area_m, 3072, KD, P)
        y_pair = carve(area_m, 4096, D)
        place_T = carve(area_m, 5120, T, P)
        place_bf = carve(area_m, 5376, T, P, dt=BF16)
        place_g = carve(area_m, 5504, T, P)
        r_lg = carve(area_m, 5760, T, E)
        r_top = carve(area_m, 5824, T, 8)
        r_idx = carve(area_m, 5840, T, 8, dt=U32)
        r_idf = carve(area_m, 5856, T, 8)
        r_p = carve(area_m, 5872, T, 8)
        r_s = carve(area_m, 5888, 8)
        r_eq = carve(area_m, 5896, T * TOP_K, E)
        r_eqp = carve(area_m, 6152, T * TOP_K, E)
        r_sel = carve(area_m, 6408, T, E, dt=BF16)
        r_pos = carve(area_m, 6440, T, E)
        r_iota = carve(area_m, 6504, E)
        o_T = carve(area_m, 6536, 2 * T, P)[0:E]
        o_cnt = carve(area_m, 7048, MAX_OVER)[0:E]
        o_cbf = carve(area_m, 7064, MAX_OVER, dt=BF16)[0:E]
        o_a = carve(area_m, 7072, MAX_OVER)[0:E]
        o_b = carve(area_m, 7088, MAX_OVER)[0:E]
        o_sel = carve(area_m, 7104, 2, MAX_OVER)[0:E]
        o_blk = carve(area_m, 7136, MAX_OVER)[0:E]
        o_j = carve(area_m, 7152, MAX_OVER)[0:E]
        o_e = carve(area_m, 7168, 1)[0:E]
        o_neg = carve(area_m, 7172, P)[0:E]
        o_row = carve(area_m, 7300, 2 * MAX_OVER + 2)[0:1]
        lgT = carve(area_m, 3072, S)
        glu = carve(area_x, 0, FH)
        lin = carve(area_x, 512, FH)
        sig = carve(area_x, 1024, FH)
        actT = carve(area_x, 1536, FH // P, P)

        bank = [ctx.enter_context(nc.psum_tensor(f"bank{i}", [P, 512], F32)) for i in range(8)]
        acc, (glu_b, lin_b, y_b, t_b) = bank[0:4], bank[4:8]

        s_x = [sem(f"x_loaded{t}") for t in range(T)]
        s_small, s_rw = sem("small_loaded"), sem("gains_loaded")
        s_bias = sem("biases_loaded")
        BLOCKS = ["q", "k", "v", "u", "gp0", "gp1", "pool_up", "ga0", "ga1", "attn_up", "out0", "out1"]
        s_load = [[sem(f"raw{j}_half{h}_loaded") for h in range(2)] for j in range(NRAW)]
        s_hi, s_lo = sem("first_parts_done"), sem("rests_done")
        s_unit, s_ev, s_ga = sem("unit_done"), sem("unit_evacuated"), sem("attn_gate_ready")
        s_sigp, s_half, s_mf, s_mhi = sem("pool_gate_ready"), sem("mix_hi"), sem("merged_sum"), sem("merged_hi")
        s_const = sem("constants_done")
        s_pool = sem("pool_order")
        s_dve, s_dve2 = sem("dve_order"), sem("dve_loop_order")
        s_act = sem("act_order")
        s_sumsq, s_mean, s_rstd = sem("sumsq_done"), sem("mean_done"), sem("rstd_done")
        s_xn, s_xT, s_hTh, s_hT = sem("xn_ready"), sem("x_transposed"), sem("hT_hi"), sem("hT_ready")
        s_rows, s_cols = sem("rows_transposed"), sem("cols_ready")
        s_proj, s_first = sem("projected"), sem("first_half_projected")
        s_qkn, s_vn, s_tr, s_qk = sem("qk_normed"), sem("v_ready"), sem("qk_transposed"), sem("qk_ready")
        s_kz0 = sem("kz_zeroed")
        s_dT = sem("pool_diff_ready")
        s_z, s_ln, s_sp = sem("scores_done"), sem("ln_done"), sem("softplus_done")
        s_acc, s_prob, s_o = sem("logprob_done"), sem("prob_done"), sem("attn_done")
        s_oh, s_oT, s_mrg = sem("attnT_hi"), sem("attnT_ready"), sem("merged_ready")
        s_wo, s_x1, s_hn = sem("out_proj_done"), sem("x1_ready"), sem("hn_ready")
        s_hnT, s_hT2, s_hT3 = sem("x1_transposed"), sem("router_in_by_dve"), sem("router_in_by_act")
        s_lgT, s_lgTs, s_lg = sem("logitsT_done"), sem("logitsT_ready"), sem("logits_done")
        s_soft, s_softe = sem("softmax_in"), sem("softmax_exp")
        s_sel, s_cnt = sem("selection_ready"), sem("ranks_done")
        s_p1, s_rest, s_parts = sem("part_cast"), sem("rest_ready"), sem("parts_ready")
        s_tab, s_tabv = sem("table_matmuls"), sem("table_steps")
        s_bready = sem("biases_split")
        s_oTT = sem("by_expert_ready")
        s_table, s_ids = sem("pairs_counted"), sem("experts_listed")
        s_sela, s_selb = sem("selector_a_ready"), sem("selector_b_ready")
        s_gl = [sem(f"gate_loaded{i}") for i in range(NSLOT)]
        s_dl = [sem(f"down_loaded{i}") for i in range(NDOWN)]
        s_gu, s_du = sem("gate_slots_used"), sem("down_slots_used")
        s_sr, s_glu, s_sig = sem("swiglu_read"), sem("glu_ready"), sem("sigmoid_ready")
        s_actr, s_aps, s_actT = sem("act_ready"), sem("act_transposed"), sem("actT_ready")
        s_y, s_comb = sem("y_ready"), sem("combined")
        s_onehot = sem("one_hot_ready")
        s_place, s_ptp, s_pt = sem("places_ready"), sem("places_transposed"), sem("placeT_ready")
        s_gps, s_gev = sem("gathered"), sem("gather_ready")
        s_final, s_outv, s_outa, s_store = sem("sum_done"), sem("out_by_dve"), sem("out_by_act"), sem("out_stored")

        block = ctx.enter_context(nc.Block())

        col_of = {"u": 0, "q": 1, "k": 2, "v": 3, "gp0": 4, "gp1": 5, "ga0": 6, "ga1": 7}
        ROW_G1, ROW_G2, ROW_PS, ROW_Q, ROW_K = 0, KD, 2 * KD, 2 * KD + G, 2 * KD + G + 1
        NROWS = ROW_K + 1

        UNITS = [("u", 0), ("u", 1), ("gp0", 0), ("gp0", 1), ("mix", 0), ("mix", 1), ("gp1", 0), ("gp1", 1)] \
            + [("pool_up", j) for j in range(4)] + [("ga0", 0), ("ga0", 1), ("ga1", 0), ("ga1", 1)] \
            + [("attn_up", j) for j in range(4)]
        STEP = {0: 0, 1: 1, 2: 2, 3: 3, 6: 4, 7: 5}

        def used(b, h):
            if BLOCKS[b] in ("q", "k", "v"):
                return (s_first, b + 1) if h == 0 else (s_proj, 2 * b + 2)
            if BLOCKS[b] in ("out0", "out1"):
                return (s_first, b - 6) if h == 0 else (s_wo, 2 * b - 18)
            unit = UNITS.index((BLOCKS[b], 0))
            if BLOCKS[b] in ("pool_up", "attn_up"):
                return s_unit, unit + 2 * h + 2
            return s_unit, unit + h + 1

        BOTH, ONE, TWO = slice(0, 2), slice(0, 1), slice(1, 2)
        HI_OF = {0: (4, BOTH), 3: (5, ONE), 5: (5, TWO), 6: (6, BOTH), 8: (7, BOTH), 12: (8, BOTH), 14: (9, BOTH),
                 15: (10, ONE), 16: (10, TWO)}
        LO_OF = {0: (4, BOTH), 3: (5, ONE), 5: (5, TWO), 6: (6, BOTH), 9: (7, ONE), 10: (7, TWO), 12: (8, BOTH),
                 14: (9, BOTH), 15: (10, ONE)}

        def pieces(b):
            n = 4 if b == 0 else 2
            before = 0 if b == 0 else 4 + 2 * (b - 1)
            return [(i * BW // n, BW // n, before + i + 1) for i in range(n)]

        def unit_wait(eng, n):
            if UNITS[n][0].startswith("ga"):
                eng.wait_ge(s_ga, n - 11)
            else:
                eng.wait_ge(s_ev, n + 1 if n < 12 else n - 3)

        PROJ = (6, 2, 4)
        TR = (0, 6)

        def head_bank(h):
            return 2 * (h // 2 % 3) + h % 2

        SLOT = ((4, 5, 6, 7, 8, 9, 10, 11), (0, 12, 1, 13, 2, 14, 3, 15))

        @block.sync
        def _(sp):
            for t in range(T):
                sp.dma_start(x_sb[:, t], x_t[:, t]).then_inc(s_x[t], 16)

            def load_block(b):
                n = BLOCKS[b]
                if n in col_of:
                    src = w_in_b[col_of[n]]
                elif n.startswith("out"):
                    src = w_out[0].rearrange("(k p) (b n) -> b p k n", p=P, n=BLK)[int(n[3])]
                else:
                    src = {"pool_up": w_pool_up, "attn_up": w_attn_up}[n][0].rearrange("(k p) n -> p k n", p=P)
                cn = src.shape[2] // 2
                for h in range(2):
                    if b >= NRAW:
                        sp.wait_ge(*used(b - NRAW, h))
                    sp.dma_start(raw[b % NRAW][:, h * HW:(h + 1) * HW].rearrange("p (k n) -> p k n", n=cn),
                                 src[:, :, h * cn:(h + 1) * cn]).then_inc(s_load[b % NRAW][h], 16)

            for r, src in ((ROW_G1, norm1_g), (ROW_G2, norm2_g), (ROW_PS, pool_scale)):
                n = src.shape[1] // P
                sp.dma_start(rows[r:r + n, :], src[0].rearrange("(k p) -> k p", p=P)).then_inc(s_rw, 16)
            load_block(0)
            sp.dma_start(grp_w, w_pool_grp[0].rearrange("g c d -> c g d")).then_inc(s_small, 16)
            for b in range(1, NRAW):
                load_block(b)
            sp.dma_start(router_w[:], w_router[0].rearrange("(k p) e -> p k e", p=P)).then_inc(s_small, 16)
            sp.dma_start(router_b[:], b_router[0:1, :].to_broadcast([P, E])).then_inc(s_small, 16)
            for b in range(NRAW, len(BLOCKS)):
                if b == 10:
                    sp.wait_ge(s_o, HEADS)
                    sp.dma_start(stage_up, b_gate_up[0]).then_inc(s_bias, 16)
                    sp.dma_start(stage_down, b_down[0]).then_inc(s_bias, 16)
                load_block(b)

            def load_gate(e, half, c):
                s = SLOT[half][c]
                sp.dma_start(gate_ring[:, s, :], w_gate_up[0, e, c * P:(c + 1) * P, :]).then_inc(s_gl[s], 16)

            def load_gate_at(e, half, c):
                s = SLOT[half][c]
                sp.dma_start(gate_ring[:, s, :],
                             w_gate_up[0, bass.ds(e, 1), c * P:(c + 1) * P, :].rearrange("a p n -> (a p) n")) \
                  .then_inc(s_gl[s], 16)

            def load_down(e, c):
                sp.dma_start(down_ring[:, c], w_down[0, e, 2 * c * P:2 * (c + 1) * P, :]
                             .rearrange("(k p) n -> p k n", p=P)).then_inc(s_dl[c], 16)

            def down_src(e, c):
                return w_down[0, bass.ds(e, 1), 2 * c * P:2 * (c + 1) * P, :] \
                    .rearrange("a (k p) n -> p (a k) n", p=P)

            for c in range(KD):
                if c < 6:
                    sp.wait_ge(*used(7 + c // 2, c % 2))
                load_gate(0, 0, c)
            for c in range(KD):
                if c % 2 == 0:
                    sp.wait_ge(*used(10 + c // 4, c // 2 % 2))
                load_gate(1, 1, c)
            sp.wait_ge(s_bready, 1)
            load_down(0, 3)
            sp.wait_ge(s_lgT, 1)
            load_down(0, 0)
            sp.wait_ge(s_hn, T)
            sp.wait_ge(s_p1, T)
            load_down(0, 2)
            sp.wait_ge(s_parts, T)
            load_down(0, 1)
            with sp.Fori(1, EARLY) as i:
                for half in range(2):
                    for c in range(KD):
                        sp.wait_ge(s_gu, (i - 1) * (2 * KD) + (half * KD + c + 1))
                        load_gate_at(2 * i + half, half, c)
                    for c in range(NDOWN):
                        sp.wait_ge(s_du, (i - 1) * (2 * NDOWN) + (half * NDOWN + c + 1))
                        sp.dma_start(down_ring[:, c], down_src(2 * i + half - 1, c)).then_inc(s_dl[c], 16)
            for c in range(NDOWN):
                sp.wait_ge(s_du, (2 * EARLY - 2) * NDOWN + c + 1)
                load_down(2 * EARLY - 1, c)
            sp.wait_ge(s_ids, 1)
            pairs = sp.value_load(item_table[0:1, COLS:COLS + 1], min_val=E // 2, max_val=ITEMS // 2)
            with sp.Fori(EARLY, pairs) as i:
                for half in range(2):
                    e = sp.value_load(item_table[0:1, bass.ds(2 * i + half, 1)], min_val=0, max_val=E - 1)
                    for c in range(KD):
                        sp.wait_ge(s_gu, (i - 1) * (2 * KD) + (half * KD + c + 1))
                        load_gate_at(e, half, c)
                    for c in range(NDOWN):
                        sp.wait_ge(s_du, i * (2 * NDOWN) + ((half - 1) * NDOWN + c + 1))
                        sp.dma_start(down_ring[:, c], down_src(e, c)).then_inc(s_dl[c], 16)
            for t in range(T):
                for n in range(2):
                    sp.wait_ge((s_outv, s_outa)[n], t + 1)
                    sp.dma_start(out_t[t, :, n * FH:(n + 1) * FH], gate_ring[:, 2 * t + n, 0:FH]) \
                      .then_inc(s_store, 16)
            sp.wait_ge(s_store, 16 * 2 * T)

        @block.gpsimd
        def _(pool):
            order = [0]

            def link(ins):
                order[0] += 1
                ins.then_inc(s_pool, 1)
                pool.wait_ge(s_pool, order[0])

            consts = [0]

            def const(ins):
                consts[0] += 1
                ins.then_inc(s_const, 1)
                pool.wait_ge(s_const, consts[0])

            def select(view, compare, fill, mult=1, step=-1, base=0, n=P):
                return nc.gpsimd.affine_select(out=view, in_=view, compare_op=compare, fill=fill, base=base,
                                               pattern=[[step, n]], channel_multiplier=mult)

            def power(dst, src, n):
                return nc.gpsimd.tensor_tensor(dst, src, tiny[:, 62:63].to_broadcast([P, n]), ALU.pow)

            link(nc.gpsimd.memset(ident[:], 0.0))
            const(select(ident[:], ALU.not_equal, 1.0))
            link(nc.gpsimd.memset(tiny[:, 62:63], -0.5))
            pool.wait_ge(s_mean, 1)
            power(tiny[:, 4:6], tiny[:, 2:4], T).then_inc(s_rstd, 1)
            pool.wait_ge(s_rstd, 1)
            link(nc.gpsimd.memset(mask_bf, 0.0))
            const(select(mask_bf, ALU.is_gt, MASKED, mult=-1, step=1))
            link(nc.gpsimd.memset(ident_bf, 0.0))
            const(select(ident_bf, ALU.not_equal, 1.0))
            link(nc.gpsimd.memset(from_key, -1.0))
            const(select(from_key, ALU.is_ge, 0.0))
            const(nc.gpsimd.memset(minus, -1.0))
            const(nc.gpsimd.memset(ones_bf[:], 1.0))
            link(nc.gpsimd.memset(below_bf[:], 1.0))
            const(select(below_bf[:], ALU.is_gt, 0.0, mult=-1, step=1))
            const(nc.gpsimd.iota(iota64[:], pattern=[[1, SLOTS]], base=0, channel_multiplier=0,
                                 allow_small_or_imprecise_dtypes=True))
            link(nc.gpsimd.memset(item_sel[:], 0.0))
            for part in range(3):
                v = item_sel[part * E:(part + 1) * E, 0:E]
                const(select(v, ALU.not_equal, 1.0, n=E))
            const(nc.gpsimd.iota(item_table[:], pattern=[[1, COLS + 2]], base=0, channel_multiplier=0))
            pool.wait_ge(s_xT, 1)
            nc.gpsimd.memset(kz, 0.0).then_inc(s_kz0, 1)
            pool.wait_ge(s_kz0, 1)
            for n in range(2):
                pool.wait_ge(s_mean, 2 + n)
                power(tiny[:, 16 + 16 * n:32 + 16 * n], tiny[:, 16 + 16 * n:32 + 16 * n], 2 * HEADS) \
                    .then_inc(s_rstd, 1)
                pool.wait_ge(s_rstd, 2 + n)
            pool.wait_ge(s_mean, 4)
            power(tiny[:, 4:6], tiny[:, 2:4], T).then_inc(s_rstd, 1)
            pool.wait_ge(s_rstd, 4)
            pool.wait_ge(s_wo, 2 * T)
            pool.wait_ge(s_bready, 1)
            const(nc.gpsimd.iota(r_iota, pattern=[[1, E]], base=0, channel_multiplier=0,
                                 allow_small_or_imprecise_dtypes=True))
            const(nc.gpsimd.iota(o_j, pattern=[[1, MAX_OVER]], base=0, channel_multiplier=0,
                                 allow_small_or_imprecise_dtypes=True))
            const(nc.gpsimd.iota(o_e, pattern=[[0, 1]], base=0, channel_multiplier=1,
                                 allow_small_or_imprecise_dtypes=True))
            const(nc.gpsimd.memset(o_neg, -float(SLOTS)))
            const(nc.gpsimd.memset(place_T, 0.0))
            nc.gpsimd.memset(y_pair, 0.0).then_inc(s_y, 1)
            pool.wait_ge(s_y, 1)
            for t in range(T):
                pool.wait_ge(s_p1, T + t + 1)
                nc.gpsimd.tensor_tensor(parts[:, t, 2 * D:3 * D], rest[:, t], parts[:, t, D:2 * D], ALU.subtract) \
                    .then_inc(s_parts, 1)
                pool.wait_ge(s_parts, t + 1)

        N_CONST = 17

        @block.scalar
        def _(act):
            for r, src in ((ROW_Q, q_norm_g), (ROW_K, k_norm_g)):
                for half in range(2):
                    act.dma_start(rows[r:r + 1, half * HD:(half + 1) * HD], src).then_inc(s_rw, 16)

            for t in range(T):
                act.wait_ge(s_x[t], 16)
                last = nc.scalar.activation(hT.rearrange("p a b -> p (a b)")[:, t * D:(t + 1) * D], x_sb[:, t],
                                            ACT.Square, accum_out=tiny[:, t:t + 1])
            last.then_inc(s_sumsq, 1)

            def split(b, which=slice(0, None)):
                for lo, n, _ in pieces(b)[which]:
                    h = lo // HW
                    if b >= NHI:
                        act.wait_ge(*used(b - NHI, h))
                    act.wait_ge(s_load[b % NRAW][h], 16 * (b // NRAW) + 16)
                    nc.scalar.activation(w_hi[b % NHI][:, lo:lo + n], raw[b % NRAW][:, lo:lo + n], ACT.Copy) \
                        .then_inc(s_hi, 1)

            split(0, slice(0, 2))
            act.wait_ge(s_cols, 1)
            act.wait_ge(s_xT, 1)
            act.wait_ge(s_mean, 1)
            for k in range(KD):
                if k == KD // 2:
                    split(0, slice(2, 3))
                nc.scalar.activation(act_in[:, 0, k, :], bank[k // 2][:, (k % 2) * S:(k % 2 + 1) * S], ACT.Copy,
                                     scale=cols[:, ROW_G1 + k:ROW_G1 + k + 1]).then_inc(s_hTh, 1)
            split(0, slice(3, 4))
            split(1)
            for n in range(2):
                for t in range(T):
                    act.wait_ge(s_proj, 1 + 2 * n + t)
                    if n:
                        act.wait_ge(s_mean, 2)
                    nc.scalar.activation(squares[:, t], bank[PROJ[n] + t][:], ACT.Square).then_inc(s_sumsq, 1)
                split(2 + n)
            for t in range(T):
                act.wait_ge(s_proj, 5 + t)
                nc.scalar.activation(vn[:, t], bank[PROJ[2] + t][:], ACT.Copy).then_inc(s_vn, 1)

            for n, (name, j) in enumerate(UNITS):
                t = STEP.get(n, -1)
                if 0 <= t - 1 < PAIRS:
                    for h in (2 * (t - 1), 2 * (t - 1) + 1):
                        act.wait_ge(s_acc, h + 1)
                        if h >= 2:
                            act.wait_ge(s_o, h - 1)
                        nc.scalar.activation(attn_prob[:, h % 2], bank[head_bank(h)][:, 0:384], ACT.Exp) \
                            .then_inc(s_prob, 1)
                if 0 <= t < PAIRS:
                    for h in (2 * t, 2 * t + 1):
                        act.wait_ge(s_z, h + 1)
                        if h >= 2:
                            act.wait_ge(s_sp, h - 1)
                        nc.scalar.activation(soft[:, h % 2], bank[head_bank(h)][:, 0:384], ACT.Abs).then_inc(s_act, 1)
                        act.wait_ge(s_act, 2 * h + 1)
                        nc.scalar.activation(soft[:, h % 2], soft[:, h % 2], ACT.Exp, scale=-1.0).then_inc(s_act, 1)
                    act.wait_ge(s_act, 4 * t + 4)
                    for h in (2 * t, 2 * t + 1):
                        nc.scalar.activation(soft[:, h % 2], soft[:, h % 2], ACT.Ln, bias=1.0).then_inc(s_ln, 1)
                if 0 <= t - 2 < PAIRS:
                    for h in (2 * (t - 2), 2 * (t - 2) + 1):
                        act.wait_ge(s_o, h + 1)
                        r = slice(h % 2 * HD, (h % 2 + 1) * HD)
                        nc.scalar.activation(mix_in[r, 1, 0, h // 2, :], bank[head_bank(h)][r, 0:S], ACT.Copy) \
                            .then_inc(s_oh, 1)
                if n == 8:
                    act.wait_ge(s_ev, 8)
                    nc.scalar.activation(gate_p.rearrange("p a b -> p (a b)"), gate_p.rearrange("p a b -> p (a b)"),
                                         ACT.Sigmoid).then_inc(s_sigp, 1)
                if n in HI_OF:
                    split(*HI_OF[n])
                if name == "mix":
                    act.wait_ge(s_unit, n + 1)
                    for g in (2 * j, 2 * j + 1):
                        nc.scalar.activation(mix_in[:, 0, 0, g, :], bank[6 + n % 2][:, (g % 2) * S:(g % 2 + 1) * S],
                                             ACT.Copy, scale=cols[:, ROW_PS + g:ROW_PS + g + 1]).then_inc(s_half, 1)
                if name.startswith("ga"):
                    act.wait_ge(s_unit, n + 1)
                    k = 4 * int(name[2]) + 2 * j
                    nc.scalar.activation(gate_a[:, k:k + 2, :], bank[6 + n % 2][:].rearrange("p (a n) -> p a n", n=S),
                                         ACT.Sigmoid).then_inc(s_ga, 1)
                if name == "attn_up":
                    act.wait_ge(s_mf, j + 1)
                    nc.scalar.activation(act_in[:, 0, 2 * j:2 * j + 2, :], gate_p[:, 2 * j:2 * j + 2, :], ACT.Copy) \
                        .then_inc(s_mhi, 1)
            split(11)

            for t in range(T):
                act.wait_ge(s_x1, t + 1)
                nc.scalar.activation(gate_p.rearrange("p a b -> p (a b)")[:, t * D:(t + 1) * D], x1[:, t], ACT.Square,
                                     accum_out=tiny[:, t:t + 1]) \
                    .then_inc(s_sumsq, 1)
            act.wait_ge(s_hnT, 1)
            for b in (1, 3):
                for k in (2 * b, 2 * b + 1):
                    nc.scalar.activation(hT[:, k, :], bank[4 + b][:, (k % 2) * S:(k % 2 + 1) * S], ACT.Copy,
                                         scale=cols[:, ROW_G2 + k:ROW_G2 + k + 1]).then_inc(s_hT3, 1)
            act.wait_ge(s_rstd, 4)
            for t in range(T):
                nc.scalar.activation(parts[:, t, 0:D], x1[:, t], ACT.Copy, scale=tiny[:, 4 + t:5 + t]) \
                    .then_inc(s_p1, 1)
            for t in range(T):
                act.wait_ge(s_rest, t + 1)
                nc.scalar.activation(parts[:, t, D:2 * D], rest[:, t], ACT.Copy).then_inc(s_p1, 1)
            act.wait_ge(s_soft, 1)
            nc.scalar.activation(r_p, r_p, ACT.Exp).then_inc(s_softe, 1)
            act.wait_ge(s_tab, 2)
            nc.scalar.activation(o_T, glu_b[0:E, :].rearrange("p (a n) -> p a n", n=P), ACT.Copy).then_inc(s_oTT, 1)

            act.wait_ge(s_table, 1)
            pairs = act.value_load(item_table[0:1, COLS:COLS + 1], min_val=E // 2, max_val=ITEMS // 2)
            with act.Fori(0, pairs) as i:
                for half in range(2):
                    act.wait_ge(s_glu, 2 * i + (half + 1))
                    nc.scalar.activation(sig, glu, ACT.Sigmoid, scale=ALPHA).then_inc(s_sig, 1)
                    if half == 0:
                        act.wait_ge(s_ptp, i + 1)
                        act.wait_ge(s_comb, i + 1)
                        nc.scalar.activation(place_T.rearrange("p a b -> p (a b)"), y_b[:, 0:T * P], ACT.Copy) \
                            .then_inc(s_pt, 1)
                    act.wait_ge(s_du, (2 * i + (half + 1)) * NDOWN)
                    for c in range(2):
                        last = nc.scalar.activation(y_pair[half * SLOTS:(half + 1) * SLOTS, c * FH:(c + 1) * FH],
                                                    y_b[c * SLOTS:(c + 1) * SLOTS, :], ACT.Copy)
                    last.then_inc(s_y, 1)
            for t in range(T):
                act.wait_ge(s_final, 2 * t + 2)
                nc.scalar.activation(gate_ring[:, 2 * t + 1, 0:FH], acc[2 * t + 1][:], ACT.Copy).then_inc(s_outa, 1)

        @block.vector
        def _(dve):
            order = [0]

            def link(ins):
                order[0] += 1
                ins.then_inc(s_dve, 1)
                dve.wait_ge(s_dve, order[0])

            def tt(o, a, b, op):
                return nc.vector.tensor_tensor(o, a, b, op)

            def mean(n, view, width):
                nc.vector.tensor_scalar(view[0], view[1], 1.0 / width, EPS, ALU.mult, ALU.add).then_inc(s_mean, 1)

            for g, w in enumerate(WINDOWS):
                for t in range(PAD):
                    if t < w:
                        nc.vector.memset(inv_count[:, g, t:t + 1], 1.0 / (t + 1))
                if w < PAD:
                    nc.vector.memset(inv_count[:, g, w:PAD], 1.0 / w)
            link(nc.vector.memset(tiny[:, 63:64], 0.0))
            dve.wait_ge(s_sumsq, 1)
            mean(0, (tiny[:, 2:4], tiny[:, 0:2]), D)
            dve.wait_ge(s_rstd, 1)
            for t in range(T):
                nc.vector.tensor_scalar(xn[:, t], x_sb[:, t], tiny[:, 4 + t:5 + t], None, ALU.mult) \
                    .then_inc(s_xn, 1)
            dve.wait_ge(s_rows, 1)
            nc.vector.tensor_copy(cols[:, 0:NROWS], bank[4][:, 0:NROWS]).then_inc(s_cols, 1)
            dve.wait_ge(s_cols, 1)

            def split(b, which=slice(0, None)):
                for lo, n, number in pieces(b)[which]:
                    dve.wait_ge(s_hi, number)
                    tt(w_lo[b % NRAW][:, lo:lo + n], raw[b % NRAW][:, lo:lo + n], w_hi_f[b % NHI][:, lo:lo + n],
                       ALU.subtract).then_inc(s_lo, 1)

            split(0, slice(0, 2))
            for k in range(KD):
                if k == KD // 2:
                    split(0, slice(2, 3))
                dve.wait_ge(s_hTh, k // 2 * 2 + 2)
                nc.vector.scalar_tensor_tensor(out=act_in[:, 1, k, :], in0=bank[k // 2][:, (k % 2) * S:(k % 2 + 1) * S],
                                               scalar=cols[:, ROW_G1 + k:ROW_G1 + k + 1],
                                               in1=act_f[:, 0, k * S:(k + 1) * S], op0=ALU.mult,
                                               op1=ALU.subtract).then_inc(s_hT, 1)
            split(0, slice(3, 4))
            split(1)

            for n, dst in enumerate((qn, kn)):
                v = tiny[:, 16 + 16 * n:32 + 16 * n]
                for t in range(T):
                    dve.wait_ge(s_sumsq, 2 + 2 * n + t)
                    link(nc.vector.tensor_reduce(v[:, t * HEADS:(t + 1) * HEADS],
                                                 squares[:, t].rearrange("p (h d) -> p h d", d=HD), AX_X, ALU.add))
                mean(1 + n, (v, v), HD)
                dve.wait_ge(s_rstd, 2 + n)
                for t in range(T):
                    tt(dst[:, t].rearrange("p (h d) -> p h d", d=HD),
                       bank[PROJ[n] + t][:].rearrange("p (h d) -> p h d", d=HD),
                       v[:, t * HEADS:(t + 1) * HEADS].unsqueeze(2).to_broadcast([P, HEADS, HD]), ALU.mult) \
                        .then_inc(s_qkn, 1)
                if n == 0:
                    split(2)
            for b in range(2):
                dve.wait_ge(s_tr, 1)
                nc.vector.tensor_scalar(qT[:, 2 * b:2 * b + 2, :],
                                        bank[TR[0] + b][:].rearrange("p (a n) -> p a n", n=S),
                                        cols[:, ROW_Q:ROW_Q + 1], float(HD) ** -0.5, ALU.mult, ALU.mult) \
                    .then_inc(s_qk, 1)
            split(3, ONE)
            dve.wait_ge(s_tr, 2)
            dve.wait_ge(s_kz0, 1)
            kz_v = kz.rearrange("p (a h) n -> p a h n", h=2)
            for b in range(2):
                for half in range(2):
                    r = slice(half * HD, (half + 1) * HD)
                    nc.vector.tensor_scalar(kz_v[r, 2 * b:2 * b + 2, half, :],
                                            bank[TR[1] + b][r, :].rearrange("p (a n) -> p a n", n=S),
                                            cols[r, ROW_K:ROW_K + 1], None, ALU.mult).then_inc(s_qk, 1)
            split(3, TWO)
            for v in (uT, sumA, sumB):
                link(nc.vector.memset(v[:, :, 0:PAD], 0.0))

            def first_half(stage, dst):
                link(nc.vector.tensor_copy(dst[0:E, :], stage))
                link(tt(stage, stage, dst[0:E, :], ALU.subtract))

            def second_half(stage, dst):
                mid = mid_part[:, 0:stage.shape[1]]
                link(nc.vector.tensor_copy(mid, stage))
                link(tt(stage, stage, mid, ALU.subtract))
                link(nc.vector.tensor_copy(dst[E:2 * E, :], mid))
                link(nc.vector.tensor_copy(dst[2 * E:3 * E, :], stage))

            for n, (name, j) in enumerate(UNITS):
                t = STEP.get(n, -1)
                if 0 <= t < PAIRS:
                    for h in (2 * t, 2 * t + 1):
                        dve.wait_ge(s_ln, h + 1)
                        if h >= 2:
                            dve.wait_ge(s_acc, h - 1)
                        nc.vector.scalar_tensor_tensor(out=spos[:, h % 2], in0=bank[head_bank(h)][:, 0:384],
                                                       scalar=0.0, in1=soft[:, h % 2], op0=ALU.max,
                                                       op1=ALU.add).then_inc(s_sp, 1)
                if 0 <= t - 2 < PAIRS:
                    for h in (2 * (t - 2), 2 * (t - 2) + 1):
                        dve.wait_ge(s_oh, h + 1)
                        r = slice(h % 2 * HD, (h % 2 + 1) * HD)
                        tt(mix_in[r, 1, 1, h // 2, :], bank[head_bank(h)][r, 0:S],
                           mix_f[r, 2, h // 2 * S:(h // 2 + 1) * S], ALU.subtract).then_inc(s_oT, 1)
                both = bank[6 + n % 2][:].rearrange("p (a n) -> p a n", n=S)
                if name == "u":
                    dve.wait_ge(s_unit, n + 1)
                    nc.vector.tensor_copy(uT[:, 2 * j:2 * j + 2, PAD:], both).then_inc(s_ev, 1)
                    if j == 1:
                        dve.wait_ge(s_ev, n + 1)
                        src = uT
                        for level in range(G):
                            dst = (sumA, sumB)[level % 2]
                            step = 1 << level
                            link(tt(dst[:, level:, PAD:], src[:, level:, PAD:], src[:, level:, PAD - step:UW - step],
                                    ALU.add))
                            src = dst
                        for g, w in enumerate(WINDOWS):
                            s = (sumA, sumB)[g % 2][:, g]
                            link(tt(s[:, 0:PAD], s[:, PAD:2 * PAD], inv_count[:, g, :], ALU.mult))
                            nc.vector.scalar_tensor_tensor(out=uT[:, g, 2 * PAD:], in0=s[:, 2 * PAD:], scalar=1.0 / w,
                                                           in1=uT[:, g, 2 * PAD:], op0=ALU.mult, op1=ALU.subtract)
                            link(tt(uT[:, g, PAD:2 * PAD], s[:, 0:PAD], uT[:, g, PAD:2 * PAD], ALU.subtract))
                        nc.vector.memset(tiny[:, 63:64], 0.0).then_inc(s_dT, 1)
                elif name.startswith("gp"):
                    dve.wait_ge(s_unit, n + 1)
                    k = 4 * int(name[2]) + 2 * j
                    nc.vector.tensor_copy(gate_p[:, k:k + 2, :], both).then_inc(s_ev, 1)
                elif name == "mix":
                    for g in (2 * j, 2 * j + 1):
                        dve.wait_ge(s_half, 2 * j + 2)
                        last = nc.vector.scalar_tensor_tensor(
                            out=mix_in[:, 0, 1, g, :], in0=both[:, g % 2], scalar=cols[:, ROW_PS + g:ROW_PS + g + 1],
                            in1=mix_f[:, 0, g * S:(g + 1) * S], op0=ALU.mult, op1=ALU.subtract)
                    last.then_inc(s_ev, 1)
                elif name == "pool_up":
                    dve.wait_ge(s_sigp, 1)
                    dve.wait_ge(s_unit, n + 1)
                    v = gate_p[:, 2 * j:2 * j + 2, :]
                    tt(v, both, v, ALU.mult).then_inc(s_ev, 1)
                elif n == 13:
                    dve.wait_ge(s_bias, 32)
                    first_half(stage_down, bias_down)
                    second_half(stage_down, bias_down)
                elif n == 15:
                    first_half(stage_up, bias_up)
                elif name == "attn_up":
                    dve.wait_ge(s_unit, n + 1)
                    dve.wait_ge(s_ga, 4)
                    v, m = gate_a[:, 2 * j:2 * j + 2, :], gate_p[:, 2 * j:2 * j + 2, :]
                    tt(v, both, v, ALU.mult).then_inc(s_ev, 1)
                    dve.wait_ge(s_ev, n - 3)
                    tt(m, m, v, ALU.add).then_inc(s_mf, 1)
                    dve.wait_ge(s_mhi, j + 1)
                    dve.wait_ge(s_mf, j + 1)
                    tt(act_in[:, 1, 2 * j:2 * j + 2, :], m, carve(act_f[:, 0, :], 2 * j * S, 2, S), ALU.subtract) \
                        .then_inc(s_mrg, 1)
                if n in LO_OF:
                    split(*LO_OF[n])
            split(10, TWO)
            split(11)

            second_half(stage_up, bias_up)
            nc.vector.memset(tiny[:, 63:64], 0.0).then_inc(s_bready, 1)

            for n in range(2):
                for t in range(T):
                    dve.wait_ge(s_wo, 2 * n + t + 1)
                    last = tt(x1[:, t, n * FH:(n + 1) * FH], acc[2 * t + n][:], x_sb[:, t, n * FH:(n + 1) * FH],
                              ALU.add)
                    if n == 1:
                        last.then_inc(s_x1, 1)
            dve.wait_ge(s_sumsq, 7)
            mean(3, (tiny[:, 2:4], tiny[:, 0:2]), D)
            dve.wait_ge(s_hnT, 1)
            for b in (0, 2):
                tt(hT[:, 2 * b:2 * b + 2, :], bank[4 + b][:].rearrange("p (a n) -> p a n", n=S),
                   cols[:, ROW_G2 + 2 * b:ROW_G2 + 2 * b + 2].unsqueeze(2).to_broadcast([P, 2, S]), ALU.mult) \
                    .then_inc(s_hT2, 1)
            dve.wait_ge(s_rstd, 4)
            for t in range(T):
                nc.vector.tensor_scalar(rest[:, t], x1[:, t], tiny[:, 4 + t:5 + t], None, ALU.mult).then_inc(s_hn, 1)
            dve.wait_ge(s_lgT, 1)
            nc.vector.tensor_copy(lgT, bank[4][:, 0:S]).then_inc(s_lgTs, 1)
            for t in range(T):
                dve.wait_ge(s_hn, t + 1)
                dve.wait_ge(s_p1, t + 1)
                tt(rest[:, t], rest[:, t], parts[:, t, 0:D], ALU.subtract).then_inc(s_rest, 1)
            dve.wait_ge(s_lg, 1)
            link(nc.vector.tensor_reduce(r_lg, bank[5][:, 0:T * P].rearrange("p (t c e) -> p t e c", c=COLT, e=E),
                                         AX_X, ALU.add))
            for t in range(T):
                last = nc.vector.scalar_tensor_tensor(out=r_lg[:, t], in0=r_lg[:, t],
                                                      scalar=tiny[:, 4 + t:5 + t], in1=router_b[:], op0=ALU.mult,
                                                      op1=ALU.add)
            link(last)
            for t in range(T):
                link(nc.vector.max(r_top[:, t], r_lg[:, t]))
            for t in range(T):
                last = nc.vector.max_index(r_idx[:, t], r_top[:, t], r_lg[:, t])
            link(last)
            tt(r_p, r_top, r_top[:, :, 0:1].to_broadcast([P, T, 8]), ALU.subtract).then_inc(s_soft, 1)
            link(nc.vector.tensor_copy(r_idf, r_idx))
            dve.wait_ge(s_const, N_CONST)
            eq4 = r_eq.rearrange("p (t r) e -> p t r e", r=TOP_K)
            eqp4 = r_eqp.rearrange("p (t r) e -> p t r e", r=TOP_K)
            for t in range(T):
                last = tt(eq4[:, t], r_iota.unsqueeze(1).to_broadcast([P, TOP_K, E]),
                          r_idf[:, t, 0:TOP_K].unsqueeze(2).to_broadcast([P, TOP_K, E]), ALU.is_equal)
            link(last)
            with nc.allow_low_precision(reason="sums of four zeros and ones, at most one of them a one"):
                nc.vector.tensor_reduce(r_sel, eq4.rearrange("p t r e -> p t e r"), AX_X, ALU.add).then_inc(s_sel, 1)
            dve.wait_ge(s_cnt, 1)
            link(nc.vector.scalar_tensor_tensor(out=r_pos, in0=bank[6][:, 0:T * E].rearrange("p (t e) -> p t e", e=E),
                                                scalar=FAR, in1=r_sel, op0=ALU.add, op1=ALU.mult))
            nc.vector.memset(pos_item[:, :, ITEMS:], -FAR)
            nc.vector.memset(gate_item[:, :, ITEMS:], 0.0)
            link(nc.vector.tensor_scalar(pos_item[:, :, 0:E], r_pos, FAR, None, ALU.subtract))

            def places(at):
                iota4 = iota64[:].unsqueeze(1).to_broadcast([P, 2, SLOTS])
                for t in range(T):
                    tt(place_bf[:, t].rearrange("p (j s) -> p j s", s=SLOTS), iota4,
                       pos_item[:, t, at].unsqueeze(2).to_broadcast([P, 2, SLOTS]), ALU.is_equal) \
                        .then_inc(s_onehot, 1)
                return at

            def gated(at):
                for t in range(T):
                    last = tt(place_g[:, t].rearrange("p (j s) -> p j s", s=SLOTS),
                              place_bf[:, t].rearrange("p (j s) -> p j s", s=SLOTS),
                              gate_item[:, t, at].unsqueeze(2).to_broadcast([P, 2, SLOTS]), ALU.mult)
                last.then_inc(s_place, 1)

            def selector(half, col, signal):
                nc.vector.tensor_copy(sel_item[:, half, :], item_sel[:, col].to_broadcast([3 * E, SLOTS])) \
                    .then_inc(signal, 1)

            def evacuate_gather(r):
                src = (t_b, y_b)[r][:].rearrange("p (a n) -> p a n", n=P)
                g = cols[:, ROW_G2 + 4 * r:ROW_G2 + 4 * r + 4].unsqueeze(2).to_broadcast([P, 4, P])
                tt(hT_items[:, 4 * r:4 * r + 4, :], src, g, ALU.mult).then_inc(s_gev, 1)

            places(slice(0, 2))
            dve.wait_ge(s_softe, 1)
            link(nc.vector.tensor_reduce(r_s[:, 0:T], r_p[:, :, 0:TOP_K], AX_X, ALU.add))
            link(nc.vector.reciprocal(r_s[:, 0:T], r_s[:, 0:T]))
            link(tt(r_p, r_p, r_s[:, 0:T].unsqueeze(2).to_broadcast([P, T, 8]), ALU.mult))
            for t in range(T):
                last = tt(eqp4[:, t], eq4[:, t], r_p[:, t, 0:TOP_K].unsqueeze(2).to_broadcast([P, TOP_K, E]), ALU.mult)
            link(last)
            link(nc.vector.tensor_reduce(gate_item[:, :, 0:E], eqp4.rearrange("p t r e -> p t e r"), AX_X, ALU.add))
            dve.wait_ge(s_onehot, T)
            gated(slice(0, 2))
            selector(0, slice(0, 1), s_sela)

            cnt = lin_b[0:E, 0:MAX_OVER]
            dve.wait_ge(s_tab, 1)
            link(nc.vector.tensor_scalar(o_cnt, cnt, float(SLOTS), None, ALU.is_gt))
            for m in (2, 3):
                link(nc.vector.scalar_tensor_tensor(out=o_cnt, in0=cnt, scalar=float(m * SLOTS), in1=o_cnt,
                                                    op0=ALU.is_gt, op1=ALU.add))
            nc.vector.tensor_copy(o_cbf, o_cnt).then_inc(s_tabv, 1)
            dve.wait_ge(s_gps, 1)
            evacuate_gather(0)
            dve.wait_ge(s_tab, 2)
            link(tt(o_a, o_j, lin_b[0:E, 64:64 + MAX_OVER], ALU.subtract))
            link(tt(o_b, o_a, o_cnt, ALU.is_lt))
            link(nc.vector.scalar_tensor_tensor(out=o_sel[:, 0], in0=o_a, scalar=0.0, in1=o_b, op0=ALU.is_ge,
                                                op1=ALU.mult))
            nc.vector.scalar_tensor_tensor(out=o_blk, in0=o_a, scalar=1.0, in1=o_sel[:, 0], op0=ALU.add,
                                           op1=ALU.mult)
            nc.vector.tensor_scalar(o_sel[:, 1], o_sel[:, 0], o_e[:, 0:1], None, ALU.mult).then_inc(s_tabv, 1)
            link(nc.vector.tensor_scalar(o_row[:, 0:1], lin_b[0:1, 128:129], -1.0 / SLOTS, None, ALU.mult))
            link(nc.vector.tensor_scalar(o_row[:, 2:2 + MAX_OVER // 2],
                                         o_j[0:1, :].rearrange("p (a b) -> p b a", b=2)[:, 0, :],
                                         o_row[:, 0:1], None, ALU.is_lt))
            dve.wait_ge(s_gps, 2)
            evacuate_gather(1)
            link(nc.vector.tensor_reduce(o_row[:, 1:2], o_row[:, 2:2 + MAX_OVER // 2], AX_X, ALU.add))
            nc.vector.tensor_scalar(item_table[0:1, COLS:COLS + 1], o_row[:, 1:2], 1.0, float(E // 2),
                                    ALU.mult, ALU.add).then_inc(s_table, 1)
            nc.vector.memset(tiny[:, 63:64], 0.0).then_inc(s_sr, 1)
            for part in range(3):
                nc.vector.tensor_copy(item_sel[part * E:(part + 1) * E, E:ITEMS], o_sel[:, 0])
            dve.wait_ge(s_tab, 3)
            nc.vector.tensor_scalar(pos_item[:, :, E:ITEMS], t_b[:, 0:T * MAX_OVER]
                                    .rearrange("p (t j) -> p t j", t=T), FAR, None, ALU.subtract)
            nc.vector.tensor_copy(gate_item[:, :, E:ITEMS], t_b[:, T * MAX_OVER:2 * T * MAX_OVER]
                                  .rearrange("p (t j) -> p t j", t=T))
            row = t_b[0:1, 192:192 + MAX_OVER]
            nc.vector.tensor_scalar(item_table[0:1, E:ITEMS], row, -1.0 / SLOTS, None, ALU.mult).then_inc(s_ids, 1)

            dve.wait_ge(s_table, 1)
            pairs = dve.value_load(item_table[0:1, COLS:COLS + 1], min_val=E // 2, max_val=ITEMS // 2)
            with dve.Fori(0, pairs) as i:
                for half in range(2):
                    n1 = 2 * i + (half + 1)
                    dve.wait_ge(s_gu, n1 * KD)
                    nc.vector.tensor_scalar(glu, glu_b[:], LIMIT, None, ALU.min).then_inc(s_glu, 1)
                    nc.vector.tensor_scalar(lin, lin_b[:], LIMIT, -LIMIT, ALU.min, ALU.max).then_inc(s_sr, 1)
                    dve.wait_ge(s_glu, n1)
                    dve.wait_ge(s_sr, n1 + 1)
                    nc.vector.scalar_tensor_tensor(out=lin, in0=lin, scalar=1.0, in1=glu, op0=ALU.add,
                                                   op1=ALU.mult).then_inc(s_dve2, 1)
                    if half == 1:
                        dve.wait_ge(s_gps, 2 * i + 3)
                        evacuate_gather(0)
                    dve.wait_ge(s_dve2, n1)
                    dve.wait_ge(s_sig, n1)
                    tt(lin, lin, sig, ALU.mult).then_inc(s_actr, 1)
                    if half == 1:
                        dve.wait_ge(s_gps, 2 * i + 4)
                        evacuate_gather(1)
                    dve.wait_ge(s_aps, n1)
                    nc.vector.tensor_copy(actT, t_b[:].rearrange("p (a n) -> p a n", n=P)).then_inc(s_actT, 1)
                    if half == 0:
                        selector(1, bass.ds(2 * i + 1, 1), s_selb)
                        dve.wait_ge(s_ptp, i + 1)
                        ahead = bass.ds(2 * i + 2, 2)
                        places(ahead)
                        dve.wait_ge(s_onehot, T * i + 2 * T)
                        gated(ahead)
                    else:
                        selector(0, bass.ds(2 * i + 2, 1), s_sela)
            for t in range(T):
                dve.wait_ge(s_final, 2 * t + 1)
                nc.vector.tensor_copy(gate_ring[:, 2 * t, 0:FH], acc[2 * t][:]).then_inc(s_outv, 1)

        @block.tensor
        def _(pe):
            def mm(o, lhsT, rhs, start):
                return nc.tensor.matmul(o, lhsT, rhs, start=start, stop=True, skip_group_check=True)

            pe.wait_ge(s_const, 1)
            pe.wait_ge(s_rw, 16 * 7)
            nc.tensor.transpose(bank[4][:, 0:NROWS], rows[0:NROWS], ident[0:NROWS, 0:NROWS]).then_inc(s_rows, 1)
            pe.wait_ge(s_xn, T)
            for k in range(KD):
                for t in range(T):
                    last = nc.tensor.transpose(bank[k // 2][:, (k % 2) * S + t * P:(k % 2) * S + (t + 1) * P],
                                               xn[:, t, k * P:(k + 1) * P], ident[:])
            last.then_inc(s_xT, 1)

            def mm3(o, stat, mov, start):
                mm(o, stat[0], mov[0], start)
                mm(o, stat[0], mov[1], False)
                return mm(o, stat[1], mov[0], False)

            def weights(b, h, at, n):
                at += h * HW
                return w_hi[b % NHI][:, at:at + n], w_lo[b % NRAW][:, at:at + n]

            def acts(k, cols_at=0, n=S):
                return act_in[:, 0, k, cols_at:cols_at + n], act_in[:, 1, k, cols_at:cols_at + n]

            def wait_split(b, h):
                pe.wait_ge(s_lo, pieces(b)[h][2])

            HB = BLK // 2

            def project(b, banks, ready, done, between=None):
                for t, k in [(t, k) for k in range(KD) for t in range(T)]:
                    if t == 0:
                        ready(k)
                        if b == 0 and k % 4 == 0:
                            pe.wait_ge(s_lo, k // 4 + 1)
                        if b and k == 0:
                            wait_split(b, 0)
                    last = mm3(banks[t][:, 0:HB], acts(k, t * P, P), weights(b, 0, k * HB, HB), k == 0)
                last.then_inc(s_first, 1)
                if between:
                    between()
                for t in range(T):
                    for k in range(KD):
                        if t == 0 and b == 0 and k % 4 == 0:
                            pe.wait_ge(s_lo, k // 4 + 3)
                        if t == 0 and b and k == 0:
                            wait_split(b, 1)
                        last = mm3(banks[t][:, HB:BLK], acts(k, t * P, P), weights(b, 1, k * HB, HB), False)
                    last.then_inc(done, 1)

            def no_wait(k):
                pass

            def hT_there(k):
                pe.wait_ge(s_hT, k + 1)

            def merged_there(k):
                if k % 2 == 0:
                    pe.wait_ge(s_mrg, k // 2 + 1)

            def transposed(src, b, count):
                pe.wait_ge(s_qkn, count)
                for a in range(PAIRS):
                    for t in range(T):
                        last = nc.tensor.transpose(
                            bank[b + a // 2][:, (a % 2) * S + t * P:(a % 2) * S + (t + 1) * P],
                            src[:, t, a * P:(a + 1) * P], ident[:])
                last.then_inc(s_tr, 1)

            project(0, bank[PROJ[0]:PROJ[0] + T], hT_there, s_proj)
            project(1, bank[PROJ[1]:PROJ[1] + T], no_wait, s_proj)
            transposed(qn, TR[0], T)
            project(2, bank[PROJ[2]:PROJ[2] + T], no_wait, s_proj, lambda: transposed(kn, TR[1], 2 * T))

            pe.wait_ge(s_const, 7)
            pe.wait_ge(s_qk, 6)
            pe.wait_ge(s_vn, T)
            for n, (name, j) in enumerate(UNITS):
                t = STEP.get(n, -1)
                if 0 <= t - 2 < PAIRS:
                    pe.wait_ge(s_prob, 2 * (t - 2) + 2)
                    for key in range(T):
                        for half in range(2):
                            h = 2 * (t - 2) + half
                            o = bank[head_bank(h)][half * HD:(half + 1) * HD, :]
                            last = mm(o[:, key * P:S], vn[:, key, h * HD:(h + 1) * HD],
                                      attn_prob[:, half, key * S:(key + 1) * S - key * P], key == 0)
                            if key == T - 1:
                                last.then_inc(s_o, 1)
                if 0 <= t - 1 < PAIRS:
                    for h in (2 * (t - 1), 2 * (t - 1) + 1):
                        pe.wait_ge(s_sp, h + 1)
                        o, s = bank[head_bank(h)], spos[:, h % 2]
                        mm(o[:, 0:S + P], from_key, s, False)
                        mm(o[:, P:S], minus, s[:, S:S + P], False).then_inc(s_acc, 1)
                if 0 <= t < PAIRS:
                    if t >= 3:
                        pe.wait_ge(s_oT, 2 * (t - 3) + 2)
                    for h in (2 * t, 2 * t + 1):
                        o = bank[head_bank(h)]
                        mm(o[:, 0:S], kz[:, h, 0:P], qT[:, h // 2, :], True)
                        mm(o[:, S:S + P], kz[:, h, P:S], qT[:, h // 2, P:S], False)
                        mm(o[:, 0:P], ident_bf, mask_bf, False)
                        mm(o[:, S:S + P], ident_bf, mask_bf, False).then_inc(s_z, 1)
                if n >= 2:
                    unit_wait(pe, n - 2)
                o = bank[6 + n % 2]
                for half in range(2):
                    dst = o[:, half * S:(half + 1) * S]
                    if name == "mix":
                        if n == 4 and half == 0:
                            pe.wait_ge(s_dT, 1)
                            pe.wait_ge(s_small, 16 * 3)
                        last = mm(dst, grp_w[:, 2 * j + half, :], uT[:, 2 * j + half, PAD:], half == 0)
                        continue
                    b = BLOCKS.index(name)
                    if name in ("pool_up", "attn_up"):
                        which = name == "attn_up"
                        if j == 0 and half == 0:
                            pe.wait_ge(s_oT, HEADS) if which else unit_wait(pe, 5)
                        if j % 2 == 0 and half == 0:
                            wait_split(b, j // 2)
                        for k in range(G):
                            last = mm3(dst, weights(b, j // 2, k * FH + (j % 2 * 2 + half) * P, P),
                                       (mix_in[:, int(which), 0, k, :], mix_in[:, int(which), 1, k, :]),
                                       half == 0 and k == 0)
                        continue
                    if half == 0:
                        wait_split(b, j)
                    for k in range(KD):
                        last = mm3(dst, weights(b, j, k * HB + half * P, P), acts(k), half == 0 and k == 0)
                last.then_inc(s_unit, 1)
            for n in range(2):
                project(BLOCKS.index(f"out{n}"), [acc[n], acc[2 + n]], no_wait if n else merged_there, s_wo)
            for t in range(T):
                pe.wait_ge(s_x1, t + 1)
                for k in range(KD):
                    last = nc.tensor.transpose(bank[4 + k // 2][:, (k % 2) * S + t * P:(k % 2) * S + (t + 1) * P],
                                               x1[:, t, k * P:(k + 1) * P], ident[:])
            last.then_inc(s_hnT, 1)
            for k in range(KD):
                if k == 0:
                    pe.wait_ge(s_hT2, 2)
                    pe.wait_ge(s_hT3, 1)
                if k % 2 == 0 and k:
                    pe.wait_ge((s_hT2, s_hT3)[k // 2 % 2], (2, 2, 2, 4)[k // 2])
                c = k % COLT
                last = mm(bank[4][c * E:(c + 1) * E, 0:S], router_w[:, k, :], hT[:, k, :], k < COLT)
            last.then_inc(s_lgT, 1)
            pe.wait_ge(s_lgTs, 1)
            for t in range(T):
                last = nc.tensor.transpose(bank[5][:, t * P:(t + 1) * P], lgT[:, t * P:(t + 1) * P], ident[:])
            last.then_inc(s_lg, 1)
            pe.wait_ge(s_x1, T)
            for t in range(T):
                for n in range(2):
                    mm(acc[2 * t + n][:], ident[:], x_sb[:, t, n * FH:(n + 1) * FH], False)
            pe.wait_ge(s_sel, 1)
            mm(bank[6][:, 0:E], below_bf[:], r_sel[:, 0], True)
            mm(bank[6][:, E:2 * E], ones_bf[:], r_sel[:, 0], False)
            mm(bank[6][:, E:2 * E], below_bf[:], r_sel[:, 1], False).then_inc(s_cnt, 1)
            for t in range(T):
                last = mm(lin_b[0:E, 0:MAX_OVER], r_sel[:, t], ones_bf[:, 0:MAX_OVER], t == 0)
            last.then_inc(s_tab, 1)

            def gather(r):
                o = (t_b, y_b)[r]
                for k in range(4 * r, 4 * r + 4):
                    for t in range(T):
                        for part in range(3):
                            last = mm(o[:, (k % 4) * P:(k % 4 + 1) * P],
                                      parts[:, t, part * D + k * P:part * D + (k + 1) * P], place_bf[:, t, :],
                                      k == 4 * r and t == 0 and part == 0)
                last.then_inc(s_gps, 1)

            pe.wait_ge(s_parts, T)
            pe.wait_ge(s_onehot, T)
            gather(0)
            pe.wait_ge(s_place, 1)
            for t in range(T):
                nc.tensor.transpose(glu_b[0:E, t * P:(t + 1) * P], r_pos[:, t], ident[:])
                nc.tensor.transpose(glu_b[0:E, (T + t) * P:(T + t + 1) * P], gate_item[:, t, 0:E], ident[:])
            pe.wait_ge(s_tabv, 1)
            pe.wait_ge(s_const, N_CONST)
            mm(lin_b[0:1, 128:129], o_neg[:, 0:1], o_cnt[:, 0:1], True)
            mm(lin_b[0:E, 64:64 + MAX_OVER], below_bf[0:E, 0:E], o_cbf, False).then_inc(s_tab, 1)
            gather(1)
            pe.wait_ge(s_tabv, 2)
            pe.wait_ge(s_oTT, 1)
            pe.wait_ge(s_gev, 1)
            for t in range(T):
                v = t_b[:, t * MAX_OVER:(t + 1) * MAX_OVER]
                mm(v, o_T[:, t, :], o_sel[:, 0], t == 0)
                mm(v, o_neg, o_blk, False)
                mm(t_b[:, (T + t) * MAX_OVER:(T + t + 1) * MAX_OVER], o_T[:, T + t, :], o_sel[:, 0], False)
            mm(t_b[0:1, 192:192 + MAX_OVER], o_neg[:, 0:1], o_sel[:, 1], True).then_inc(s_tab, 1)

            def combine():
                for t in range(T):
                    for n in range(2):
                        yield mm(acc[2 * t + n][:], place_T[:, t, :], y_pair[:, n * FH:(n + 1) * FH], False)

            pe.wait_ge(s_table, 1)
            pairs = pe.value_load(item_table[0:1, COLS:COLS + 1], min_val=E // 2, max_val=ITEMS // 2)
            with pe.Fori(0, pairs) as i:
                for half in range(2):
                    n0 = 2 * i + half
                    slots = slice(half * SLOTS, (half + 1) * SLOTS)
                    if half == 0:
                        pe.wait_ge(s_gev, 2 * i + 2)
                        pe.wait_ge(s_sela, i + 1)
                    else:
                        pe.wait_ge(s_selb, i + 1)
                    pe.wait_ge(s_sr, n0 + 1)
                    for c in range(2):
                        for b, m in ((glu_b, 0), (lin_b, 1)):
                            lo = m * D + c * FH
                            mm(b[c * SLOTS:(c + 1) * SLOTS, :], sel_item[:, half, :], bias_up[:, lo:lo + FH], True)
                    for k in range(KD):
                        s = SLOT[half][k]
                        pe.wait_ge(s_gl[s], 16 * i + 16)
                        for b, m in ((glu_b, 0), (lin_b, 1)):
                            for c in range(2):
                                lo = m * D + c * FH
                                last = mm(b[c * SLOTS:(c + 1) * SLOTS, :], hT_items[:, k, slots],
                                          gate_ring[:, s, lo:lo + FH], False)
                        last.then_inc(s_gu, 1)
                    if half == 0:
                        pe.wait_ge(s_y, 2 * i + 1)
                        for last in combine():
                            pass
                        last.then_inc(s_comb, 1)
                        pe.wait_ge(s_place, i + 1)
                        for t in range(T):
                            last = nc.tensor.transpose(y_b[:, t * P:(t + 1) * P], place_g[:, t], ident[:])
                        last.then_inc(s_ptp, 1)
                    else:
                        pe.wait_ge(s_place, i + 2)
                        gather(0)
                        pe.wait_ge(s_y, 2 * i + 2)
                        gather(1)
                        pe.wait_ge(s_gev, 2 * i + 3)
                    pe.wait_ge(s_actr, n0 + 1)
                    for c in range(FH // P):
                        last = nc.tensor.transpose(t_b[:, c * P:(c + 1) * P], lin[:, c * P:(c + 1) * P], ident[:])
                    last.then_inc(s_aps, 1)
                    if half == 0:
                        pe.wait_ge(s_pt, i + 1)
                    else:
                        pe.wait_ge(s_gev, 2 * i + 4)
                    for c in range(2):
                        mm(y_b[c * SLOTS:(c + 1) * SLOTS, :], sel_item[:, half, :], bias_down[:, c * FH:(c + 1) * FH],
                           True)
                    pe.wait_ge(s_actT, n0 + 1)
                    for k in range(KD):
                        if k % 2 == 0:
                            pe.wait_ge(s_dl[k // 2], 32 * i + 16 * (half + 1))
                        f0 = (k // 4) * SLOTS
                        for c in range(2):
                            last = mm(y_b[c * SLOTS:(c + 1) * SLOTS, :], actT[:, k % 4, f0:f0 + SLOTS],
                                      down_ring[:, k // 2, k % 2, c * FH:(c + 1) * FH], False)
                        if k % 2:
                            last.then_inc(s_du, 1)
            pe.wait_ge(s_y, 2 * pairs + 1)
            for last in combine():
                last.then_inc(s_final, 1)


_INS = ["x", "norm1_g", "w_in", "q_norm_g", "k_norm_g", "w_pool_grp", "pool_scale", "w_pool_up", "w_attn_up",
        "w_out", "norm2_g", "w_router", "b_router", "w_gate_up", "b_gate_up", "w_down", "b_down"]


def kernel(**inputs):
    import numpy as _np
    import concourse.bacc as _bacc
    from concourse import mybir as _mybir
    from concourse.bass_utils import run_bass_kernel_spmd as _run

    nc = _bacc.Bacc("TRN2", target_bir_lowering=False, num_devices=1)
    arrays, args = {}, []
    for name in _INS:
        a = _np.ascontiguousarray(inputs[name])
        arrays[f"in_{name}_dram"] = a
        args.append(nc.dram_tensor(f"in_{name}_dram", a.shape, _mybir.dt.from_np(a.dtype),
                                   kind="ExternalInput").ap())
    out = nc.dram_tensor("out_0_dram", inputs["x"].shape, _mybir.dt.float32, kind="ExternalOutput").ap()
    hybrid_block_kernel(nc, *args, out)
    r = _run(nc, [arrays], core_ids=[0])
    return r.results[0]["out_0_dram"]
```
